# Optimizing a Trainium2 kernel written in Bass

```python
import math
import jax
import jax.numpy as jnp
from jax import lax
import numpy as np

D_MODEL = 1024
BATCH = 1
SEQ = 256
DEPTH = 2
DEC_BATCH = 8
DEC_SEQ = 4
PAST_LEN = 2048
PAGE_SIZE = 128

N_A_LAYERS = DEPTH // 2
N_B_LAYERS = DEPTH - N_A_LAYERS
N_DENSE = (DEPTH + 1) // 2
N_MOE = DEPTH // 2

CONV_WIDTH = 31
N_HEADS = 16
HEAD_DIM = 64
N_KV_HEADS = 4
GROUP = N_HEADS // N_KV_HEADS
BLOCK = 64
TOP_N = 16
WINDOW = 512
CMP_HIDDEN = 2 * HEAD_DIM
FORCE_SCORE = 1e4
Q_BLOCK = 32
N_BUCKETS = 32
MAX_EXACT = N_BUCKETS // 2
MAX_DISTANCE = 128
D_FF = 2816
N_EXPERTS = 8
TOP_K_EXPERTS = 2
D_FF_EXPERT = 2816
KV_SLOTS = 6
PAGED_SLOTS = 4
EPS = 1e-6
NEG = -1e30
TINY = 1e-30

kernel_name = "yoco_conformer_conv_nsa_decoder_step"

def rmsnorm(x, g):
    x32 = x.astype(jnp.float32)
    y = x32 * lax.rsqrt(jnp.mean(x32 * x32, axis=-1, keepdims=True) + EPS)
    return (y * g.astype(jnp.float32)).astype(x.dtype)

def layernorm(x, g, b):
    x32 = x.astype(jnp.float32)
    mu = jnp.mean(x32, axis=-1, keepdims=True)
    xc = x32 - mu
    y = xc * lax.rsqrt(jnp.mean(xc * xc, axis=-1, keepdims=True) + EPS)
    return (y * g.astype(jnp.float32) + b.astype(jnp.float32)).astype(x.dtype)

def rel_bucket(dist):
    n = jnp.maximum(dist, 0)
    nf = jnp.maximum(n, 1).astype(jnp.float32)
    large = MAX_EXACT + (jnp.log(nf / MAX_EXACT) / math.log(MAX_DISTANCE / MAX_EXACT)
                         * (N_BUCKETS - MAX_EXACT)).astype(jnp.int32)
    return jnp.where(n < MAX_EXACT, n, jnp.minimum(large, N_BUCKETS - 1))

def bias_2d(rel_bias, q_pos, k_pos):
    b = rel_bias.astype(jnp.float32)[rel_bucket(q_pos[:, None] - k_pos[None, :])]
    return jnp.transpose(b, (2, 0, 1)).reshape(N_KV_HEADS, GROUP, q_pos.shape[0], k_pos.shape[0])

def masked_softmax(s, mask):
    s = jnp.where(mask, s, NEG)
    m = jnp.max(s, axis=-1, keepdims=True)
    p = jnp.where(mask, jnp.exp(s - m), 0.0)
    return p / jnp.maximum(jnp.sum(p, axis=-1, keepdims=True), TINY)

def conv_module(xn, prefix, w1, b1, wdw, bdw, lng, lnb, w2, b2):
    u = xn @ w1 + b1
    u = u[..., :D_MODEL] * jax.nn.sigmoid(u[..., D_MODEL:])
    full = jnp.concatenate([prefix, u], axis=1)
    c = lax.conv_general_dilated(full, wdw[:, None, :], (1,), 'VALID',
                                 dimension_numbers=('NWC', 'WIO', 'NWC'),
                                 feature_group_count=D_MODEL) + bdw
    c = jax.nn.silu(layernorm(c, lng, lnb))
    return c @ w2 + b2, full[:, full.shape[1] - (CONV_WIDTH - 1):]

def swiglu(x, wg, wu, wd):
    return (jax.nn.silu(x @ wg) * (x @ wu)) @ wd

def moe_ffn(x, w_router, wg, wu, wd):
    B, T, D = x.shape
    xf = x.reshape(B * T, D)
    logits = (xf @ w_router).astype(jnp.float32)
    top_v, top_i = lax.top_k(logits, TOP_K_EXPERTS)
    top_w = jax.nn.softmax(top_v, axis=-1)
    combine = jnp.sum(jax.nn.one_hot(top_i, N_EXPERTS, dtype=jnp.float32) * top_w[..., None], axis=1)
    out = jnp.zeros_like(xf)
    for e in range(N_EXPERTS):
        out = out + combine[:, e:e + 1].astype(x.dtype) * swiglu(xf, wg[e], wu[e], wd[e])
    return out.reshape(B, T, D)

def compress(rows, pos_emb, w1, w2):
    B, L, KVH, dh = rows.shape
    nc = L // BLOCK
    blk = rows.reshape(B, nc, BLOCK, KVH, dh) + pos_emb[None, None, :, None, :]
    flat = jnp.transpose(blk, (0, 1, 3, 2, 4)).reshape(B, nc, KVH, BLOCK * dh)
    return jax.nn.silu(flat @ w1) @ w2

def shared_kv(h, past_kv, win_prefix, keep, norm_kv, w_kv, cmp_pos, cmp_w1, cmp_w2):
    B, T, _ = h.shape
    kv = (rmsnorm(h, norm_kv) @ w_kv).reshape(B, T, KV_SLOTS, N_KV_HEADS, HEAD_DIM)
    new_rows = kv[:, :, :PAGED_SLOTS]
    full = jnp.concatenate([past_kv, new_rows], axis=1)
    tk = full.shape[1]
    nc = tk // BLOCK
    ns = -(-tk // BLOCK)
    kc = compress(full[:, :nc * BLOCK, 0], cmp_pos[0], cmp_w1[0], cmp_w2[0])
    vc = compress(full[:, :nc * BLOCK, 1], cmp_pos[1], cmp_w1[1], cmp_w2[1])
    sel = jnp.pad(full[:, :, 2:4], ((0, 0), (0, ns * BLOCK - tk), (0, 0), (0, 0), (0, 0)))
    sel = jnp.transpose(sel.reshape(B, ns, BLOCK, 2, N_KV_HEADS, HEAD_DIM), (3, 0, 4, 1, 2, 5))
    kw_all = jnp.concatenate([win_prefix, kv[:, :, 4:]], axis=1)
    new_win = kw_all[:, kw_all.shape[1] - keep:]
    return (kc, vc, sel[0], sel[1], kw_all), new_rows, new_win

def nsa_attend(q, g, q_pos, kc, vc, ks, vs, kw, vw, kw_pos, rel_bias):
    B, Tq = q.shape[0], q.shape[1]
    f32 = jnp.float32
    nc = kc.shape[1]
    ns = ks.shape[2]
    cmp_end = jnp.arange(nc, dtype=jnp.int32) * BLOCK + (BLOCK - 1)
    s_c = jnp.einsum('bqkgd,bnkd->bkgqn', q, kc).astype(f32) + bias_2d(rel_bias, q_pos, cmp_end)
    p_c = masked_softmax(s_c, cmp_end[None, :] <= q_pos[:, None])
    o_c = jnp.einsum('bkgqn,bnkd->bqkgd', p_c.astype(vc.dtype), vc)
    imp = jnp.pad(jnp.sum(p_c, axis=2), ((0, 0), (0, 0), (0, 0), (0, ns - nc)))
    blk = jnp.arange(ns, dtype=jnp.int32)[None, :]
    cur = (q_pos // BLOCK)[:, None]
    forced = (blk == cur) | (blk == cur - 1) | (blk == 0)
    score = jnp.where(blk > cur, NEG, jnp.where(forced, FORCE_SCORE, imp))
    _, idx = lax.top_k(score, min(TOP_N, ns))
    bi = jnp.arange(B)[:, None, None, None]
    ki = jnp.arange(N_KV_HEADS)[None, :, None, None]
    k_sel = ks[bi, ki, idx].reshape(B, N_KV_HEADS, Tq, -1, HEAD_DIM)
    v_sel = vs[bi, ki, idx].reshape(B, N_KV_HEADS, Tq, -1, HEAD_DIM)
    pos_sel = (idx[..., None] * BLOCK + jnp.arange(BLOCK, dtype=jnp.int32)).reshape(B, N_KV_HEADS, Tq, -1)
    table = jnp.transpose(rel_bias.astype(f32).reshape(N_BUCKETS, N_KV_HEADS, GROUP), (1, 0, 2))
    b_s = jnp.moveaxis(table[ki, rel_bucket(q_pos[:, None] - pos_sel)], -1, 2)
    s_s = jnp.einsum('bqkgd,bkqmd->bkgqm', q, k_sel).astype(f32) + b_s
    p_s = masked_softmax(s_s, (pos_sel <= q_pos[:, None])[:, :, None])
    o_s = jnp.einsum('bkgqm,bkqmd->bqkgd', p_s.astype(v_sel.dtype), v_sel)
    d_w = q_pos[:, None] - kw_pos[None, :]
    mask_w = (d_w >= 0) & (d_w <= WINDOW) & (kw_pos[None, :] >= 0)
    s_w = jnp.einsum('bqkgd,bskd->bkgqs', q, kw).astype(f32) + bias_2d(rel_bias, q_pos, kw_pos)
    p_w = masked_softmax(s_w, mask_w)
    o_w = jnp.einsum('bkgqs,bskd->bqkgd', p_w.astype(vw.dtype), vw)
    return g[..., 0:1] * o_c + g[..., 1:2] * o_s + g[..., 2:3] * o_w

def nsa_layer(xn, w_in, w_out, ctx, rel_bias, pos0):
    B, T, _ = xn.shape
    kc, vc, ks, vs, kw_all = ctx
    wp = kw_all.shape[1] - T
    proj = xn @ w_in
    q = proj[..., :N_HEADS * HEAD_DIM].reshape(B, T, N_KV_HEADS, GROUP, HEAD_DIM) * (HEAD_DIM ** -0.5)
    g = jax.nn.sigmoid(proj[..., N_HEADS * HEAD_DIM:]).reshape(B, T, N_KV_HEADS, GROUP, 3)
    qb = Q_BLOCK if T % Q_BLOCK == 0 else T
    nb = T // qb

    def to_blocks(a):
        return jnp.moveaxis(a.reshape((B, nb, qb) + a.shape[2:]), 1, 0)

    def attend_block(args):
        q_b, g_b, start = args
        kwin = lax.dynamic_slice_in_dim(kw_all, start, qb + wp, axis=1)
        q_pos = pos0 + start + jnp.arange(qb, dtype=jnp.int32)
        kw_pos = pos0 - wp + start + jnp.arange(qb + wp, dtype=jnp.int32)
        return nsa_attend(q_b, g_b, q_pos, kc, vc, ks, vs, kwin[:, :, 0], kwin[:, :, 1], kw_pos, rel_bias)

    starts = jnp.arange(nb, dtype=jnp.int32) * qb
    o = lax.map(attend_block, (to_blocks(q), to_blocks(g), starts))
    o = jnp.moveaxis(o, 0, 1).reshape(B, T, N_HEADS * HEAD_DIM)
    return o @ w_out

def trunk(x, pos0, conv_prefix, past_kv, win_prefix, keep, p):
    h = x
    new_conv = []
    ctx, new_rows, new_win = None, None, None
    for i in range(DEPTH):
        if i == N_A_LAYERS:
            ctx, new_rows, new_win = shared_kv(h, past_kv, win_prefix, keep, p['norm_kv'], p['w_kv'],
                                               p['cmp_pos'], p['cmp_w1'], p['cmp_w2'])
        xn = rmsnorm(h, p['norm_mix'][i])
        if i < N_A_LAYERS:
            out, st = conv_module(xn, conv_prefix[i], p['conv_w_pw1'][i], p['conv_b_pw1'][i],
                                  p['conv_w_dw'][i], p['conv_b_dw'][i], p['conv_ln_g'][i],
                                  p['conv_ln_b'][i], p['conv_w_pw2'][i], p['conv_b_pw2'][i])
            new_conv.append(st)
        else:
            j = i - N_A_LAYERS
            out = nsa_layer(xn, p['nsa_w_in'][j], p['nsa_w_out'][j], ctx, p['rel_bias'], pos0)
        h = h + out
        xn = rmsnorm(h, p['norm_ffn'][i])
        if i % 2 == 0:
            e = i // 2
            h = h + swiglu(xn, p['ffn_w_gate'][e], p['ffn_w_up'][e], p['ffn_w_down'][e])
        else:
            e = i // 2
            h = h + moe_ffn(xn, p['moe_w_router'][e], p['moe_w_gate'][e], p['moe_w_up'][e], p['moe_w_down'][e])
    return rmsnorm(h, p['norm_final']), new_rows, new_win, jnp.stack(new_conv)

def setup_inputs(seed: int = 0) -> dict:
    key = jax.random.key(seed)
    ks = jax.random.split(key, 40)
    f32 = jnp.float32

    def nrm(k, shape, scale):
        return scale * jax.random.normal(k, shape, f32)

    D = D_MODEL
    HD = N_HEADS * HEAD_DIM
    n_pages = PAST_LEN // PAGE_SIZE
    n_used = DEC_BATCH * n_pages
    n_phys = n_used + max(1, n_used // 4)
    w_buf = min(WINDOW, PAST_LEN)
    page_table = jax.random.permutation(ks[0], n_phys)[:n_used].reshape(DEC_BATCH, n_pages).astype(jnp.int32)
    return {
        'x_prompt': nrm(ks[1], (BATCH, SEQ, D), 1.0),
        'x_sample': nrm(ks[2], (DEC_BATCH, DEC_SEQ, D), 1.0),
        'cache_kv': nrm(ks[3], (n_phys, PAGE_SIZE, PAGED_SLOTS, N_KV_HEADS, HEAD_DIM), 1.0),
        'state_win_kv': nrm(ks[4], (DEC_BATCH, w_buf, 2, N_KV_HEADS, HEAD_DIM), 1.0),
        'state_conv': nrm(ks[5], (N_A_LAYERS, DEC_BATCH, CONV_WIDTH - 1, D), 0.5),
        'page_table': page_table,
        'norm_mix': 1.0 + nrm(ks[6], (DEPTH, D), 0.02),
        'norm_ffn': 1.0 + nrm(ks[7], (DEPTH, D), 0.02),
        'norm_kv': 1.0 + nrm(ks[8], (D,), 0.02),
        'norm_final': 1.0 + nrm(ks[9], (D,), 0.02),
        'conv_w_pw1': nrm(ks[10], (N_A_LAYERS, D, 2 * D), D ** -0.5),
        'conv_b_pw1': nrm(ks[11], (N_A_LAYERS, 2 * D), 0.02),
        'conv_w_dw': nrm(ks[12], (N_A_LAYERS, CONV_WIDTH, D), CONV_WIDTH ** -0.5),
        'conv_b_dw': nrm(ks[13], (N_A_LAYERS, D), 0.02),
        'conv_ln_g': 1.0 + nrm(ks[14], (N_A_LAYERS, D), 0.02),
        'conv_ln_b': nrm(ks[15], (N_A_LAYERS, D), 0.02),
        'conv_w_pw2': nrm(ks[16], (N_A_LAYERS, D, D), D ** -0.5),
        'conv_b_pw2': nrm(ks[17], (N_A_LAYERS, D), 0.02),
        'w_kv': nrm(ks[18], (D, KV_SLOTS * N_KV_HEADS * HEAD_DIM), D ** -0.5),
        'cmp_pos': nrm(ks[19], (2, BLOCK, HEAD_DIM), 0.1),
        'cmp_w1': nrm(ks[20], (2, BLOCK * HEAD_DIM, CMP_HIDDEN), (BLOCK * HEAD_DIM) ** -0.5),
        'cmp_w2': nrm(ks[21], (2, CMP_HIDDEN, HEAD_DIM), CMP_HIDDEN ** -0.5),
        'nsa_w_in': nrm(ks[22], (N_B_LAYERS, D, HD + 3 * N_HEADS), D ** -0.5),
        'nsa_w_out': nrm(ks[23], (N_B_LAYERS, HD, D), HD ** -0.5),
        'rel_bias': nrm(ks[24], (N_BUCKETS, N_HEADS), 0.5),
        'ffn_w_gate': nrm(ks[25], (N_DENSE, D, D_FF), D ** -0.5),
        'ffn_w_up': nrm(ks[26], (N_DENSE, D, D_FF), D ** -0.5),
        'ffn_w_down': nrm(ks[27], (N_DENSE, D_FF, D), D_FF ** -0.5),
        'moe_w_router': nrm(ks[28], (N_MOE, D, N_EXPERTS), D ** -0.5),
        'moe_w_gate': nrm(ks[29], (N_MOE, N_EXPERTS, D, D_FF_EXPERT), D ** -0.5),
        'moe_w_up': nrm(ks[30], (N_MOE, N_EXPERTS, D, D_FF_EXPERT), D ** -0.5),
        'moe_w_down': nrm(ks[31], (N_MOE, N_EXPERTS, D_FF_EXPERT, D), D_FF_EXPERT ** -0.5),
    }

def reference(x_prompt, x_sample, cache_kv, state_win_kv, state_conv, page_table,
              norm_mix, norm_ffn, norm_kv, norm_final,
              conv_w_pw1, conv_b_pw1, conv_w_dw, conv_b_dw, conv_ln_g, conv_ln_b, conv_w_pw2, conv_b_pw2,
              w_kv, cmp_pos, cmp_w1, cmp_w2, nsa_w_in, nsa_w_out, rel_bias,
              ffn_w_gate, ffn_w_up, ffn_w_down,
              moe_w_router, moe_w_gate, moe_w_up, moe_w_down):
    p = dict(norm_mix=norm_mix, norm_ffn=norm_ffn, norm_kv=norm_kv, norm_final=norm_final,
             conv_w_pw1=conv_w_pw1, conv_b_pw1=conv_b_pw1, conv_w_dw=conv_w_dw, conv_b_dw=conv_b_dw,
             conv_ln_g=conv_ln_g, conv_ln_b=conv_ln_b, conv_w_pw2=conv_w_pw2, conv_b_pw2=conv_b_pw2,
             w_kv=w_kv, cmp_pos=cmp_pos, cmp_w1=cmp_w1, cmp_w2=cmp_w2,
             nsa_w_in=nsa_w_in, nsa_w_out=nsa_w_out, rel_bias=rel_bias,
             ffn_w_gate=ffn_w_gate, ffn_w_up=ffn_w_up, ffn_w_down=ffn_w_down,
             moe_w_router=moe_w_router, moe_w_gate=moe_w_gate, moe_w_up=moe_w_up, moe_w_down=moe_w_down)
    bp, tp, _ = x_prompt.shape
    dt = x_prompt.dtype
    conv0 = jnp.zeros((N_A_LAYERS, bp, CONV_WIDTH - 1, D_MODEL), dt)
    past0 = jnp.zeros((bp, 0, PAGED_SLOTS, N_KV_HEADS, HEAD_DIM), dt)
    win0 = jnp.zeros((bp, WINDOW, 2, N_KV_HEADS, HEAD_DIM), dt)
    y_p, kv_p, win_p, conv_p = trunk(x_prompt, 0, conv0, past0, win0, min(WINDOW, tp), p)
    bs, ts, _ = x_sample.shape
    past_len = page_table.shape[1] * cache_kv.shape[1]
    past = cache_kv[page_table].reshape(bs, past_len, PAGED_SLOTS, N_KV_HEADS, HEAD_DIM)
    y_s, kv_s, win_s, conv_s = trunk(x_sample, past_len, state_conv, past, state_win_kv,
                                     min(WINDOW, past_len + ts), p)
    return (y_p, y_s, kv_p, win_p, conv_p, kv_s, win_s, conv_s)


_drawn_inputs = setup_inputs


def setup_inputs(seed=0):
    import zlib

    import numpy as np

    out = dict(_drawn_inputs(seed))
    spreads = {}
    factors = {'norm_kv': 2.989, 'norm_final': 2.839}
    for name, (base, spread) in spreads.items():
        noise = np.random.default_rng([zlib.crc32(name.encode()), seed]).standard_normal(out[name].shape)
        drawn = base * np.exp(spread * noise) if base else spread * noise
        out[name] = jnp.asarray(drawn.astype(out[name].dtype))
    for name, factor in factors.items():
        out[name] = (out[name] * factor).astype(out[name].dtype)
    return out
```

```python
import math
from contextlib import ExitStack

import numpy as np

import concourse.bass as bass
from concourse import mybir

F32 = mybir.dt.float32
I32 = mybir.dt.int32
ALU = mybir.AluOpType
ACT = mybir.ActivationFunctionType
AXX = mybir.AxisListType.X

P = 128
D = 1024
KD = D // P
TP, NB, TS = 256, 8, 4
TSN = NB * TS
T = TP + TSN
TILES = [(0, 128), (128, 128), (256, 32)]
PAST, PAGE, NPG, NPHYS = 2048, 128, 16, 160
CW = 31
NH, HD, NKV, G = 16, 64, 4, 4
KVC = NKV * HD
BLOCK, TOPN, WIN = 64, 16, 512
NBLK = PAST // BLOCK
NSB = NBLK + 1
NBK = 32
DFF, FC = 2816, 22
NE = 8
GC = 3 * NH
EPS, NEG, TINY, FORCE = 1e-6, -1e30, 1e-30, 1e4
PAIRS = NB // 2
RING = 5
SLOT = 2048
EPAD = 35
TOE = 2 * P + P - 1


def bucket(dist):
    n = np.maximum(dist, 0)
    nf = np.maximum(n, 1).astype(np.float32)
    large = 16 + (np.log(nf / 16) / math.log(128 / 16) * 16).astype(np.int32)
    return np.where(n < 16, n, np.minimum(large, NBK - 1))


def constants():
    c = {}
    c["ident"] = np.eye(P)
    c["flip"] = np.eye(P)[::-1]
    y = np.arange(TOE)
    oh = np.zeros((NBK + 1, TOE))
    dist = 255 - y
    oh[bucket(dist)[dist >= 0], y[dist >= 0]] = 1
    oh[NBK, dist < 0] = 1
    c["oh_toe"] = oh
    q = np.arange(TP)
    ohc = np.zeros((NBK, 2, 4, P))
    mc = np.zeros((P, 2, 4))
    for qt in range(2):
        for n in range(4):
            d = q[qt * P:(qt + 1) * P] - (n * BLOCK + BLOCK - 1)
            ohc[bucket(d), qt, n, np.arange(P)] = 1
            mc[:, qt, n] = d >= 0
    c["oh_cmp_p"] = ohc.reshape(NBK, -1)
    c["mask_cmp_p"] = mc.reshape(P, -1)
    r = np.arange(P)
    rb, rh, rt = r // 64, (r // 4) % 16, r % 4

    def onehot(pos):
        m = np.zeros((4, NBK, len(pos)))
        for t in range(4):
            m[t, bucket(PAST + t - pos), np.arange(len(pos))] += 1
            m[t, NBK - 1] -= 1
        return m.reshape(P, -1)
    c["oh_smp"] = np.concatenate([onehot(np.arange(PAST - WIN, PAST)),
                                  onehot(PAST + np.arange(TSN) % TS),
                                  onehot(np.arange(NBLK) * BLOCK + BLOCK - 1)], 1)
    c["last_bucket"] = (np.arange(P) % NBK == NBK - 1).astype(float)[:, None]
    c["own_token"] = (np.arange(P)[:, None] // NBK == np.arange(4)[None]).astype(float)
    kb, kt = np.arange(TSN) // TS, np.arange(TSN) % TS
    mn = np.zeros((P, PAIRS, TSN))
    sel = np.zeros((TSN, PAIRS, P))
    for pr in range(PAIRS):
        mn[:, pr] = np.where((kb[None] == 2 * pr + rb[:, None]) & (kt[None] <= rt[:, None]), 0, NEG)
        sel[(2 * pr + rb) * TS + rt, pr, r] = 1
    c["mask_new"] = mn.reshape(P, -1)
    c["row_token"] = sel.reshape(TSN, -1)
    c["mask_win"] = np.where(np.arange(4)[None] >= rt[:, None], 0, NEG)
    c["row_head"] = (rh[:, None] == np.arange(16)[None]).astype(float)
    c["row_kv"] = (rh[:, None] // 4 == np.arange(4)[None]).astype(float)
    c["same_kv"] = ((r[:, None] // 16 == r[None] // 16) & (rt[:, None] == rt[None])).astype(float)
    i = np.arange(NSB)
    c["earlier"] = np.broadcast_to((i[None] < i[:, None]).reshape(1, -1), (P, NSB * NSB))
    c["before"] = (np.arange(P)[:, None] < np.arange(P)[None]).astype(float)
    c["iota_row"] = np.broadcast_to(np.arange(P)[None], (P, P))
    c["iota_col"] = np.arange(P)[:, None] + P * np.arange(3)[None]
    c["earlier8"] = np.broadcast_to((np.arange(8)[None] < np.arange(8)[:, None]).reshape(1, -1), (P, 64))
    c["round_off"] = np.broadcast_to(P * (np.arange(25) // 8)[None], (P, 25))
    return {k: np.ascontiguousarray(v, np.float32) for k, v in c.items()}


def build(nc, a, out):
    ctx = ExitStack()
    with ctx:
        sem_names = {}

        def sem(name):
            if name not in sem_names:
                sem_names[name] = ctx.enter_context(nc.semaphore(name))
            return sem_names[name]

        base0 = ctx.enter_context(nc.sbuf_tensor("arena", [P, ARENA // 4], F32))
        cursor = [0]

        def view(off, *shape, parts=P):
            n = int(np.prod(shape))
            assert off * 4 + n * 4 <= ARENA, (off, shape)
            v = base0[0:parts, off:off + n]
            if len(shape) == 1:
                return v
            names = "abcde"[:len(shape)]
            kw = {names[i]: shape[i] for i in range(len(shape))}
            return v.rearrange(f"p ({' '.join(names)}) -> p {' '.join(names)}", **kw)

        def take(*shape, parts=P):
            off = cursor[0]
            cursor[0] += int(np.prod(shape))
            return view(off, *shape, parts=parts)

        ring = take(RING, SLOT)
        hT = take(KD, T)
        XNT = cursor[0]
        xnT = take(KD, T)
        OT = xnT
        vec = take(96 + 248)
        ident = take(P)
        ones = take(P)
        eps = take(1)
        rstd = take(T)
        kv = take(3, 6 * KVC)
        QT = take(KD, T)
        kcT = take(2, NB, NBLK)
        vc = take(NB, KVC, parts=NBLK)
        kcTp = take(2, 4)
        vcp = take(KVC, parts=4)
        nvec = take(32)
        small = take(64)
        gsc = take(3)
        R0 = cursor[0]
        KT = take(2, 2, T)
        R1 = cursor[0]

        def phase():
            cursor[0] = R1

        phase()
        xnat = take(3, D)
        scn = take(2, D, parts=120)
        vrow = take(3, P)
        phase()
        fullP = take(KD, CW - 1 + TP)
        fullS = take(KD, NB, CW - 1 + TS)
        acc = take(KD, T)
        e0 = take(2, 2, T)
        Hf = take(FC, T)
        sqL0 = Hf[:, 0:KD, :]
        convo = Hf[:, 8:20, :].rearrange("p a b -> p (a b)")[:, 0:3 * D].rearrange("p (a b) -> p a b", a=3)
        top_l0 = cursor[0]
        tail = xnT.rearrange("p a b -> p (a b)")[:, 0:KD * 240].rearrange("p (a b) -> p a b", a=KD)
        cursor[0] = R1 + KD * (CW - 1 + TP) + KD * NB * (CW - 1 + TS) + KD * T + 4 * T
        xnat = take(3, D)
        scn = take(2, D, parts=120)
        vrow = take(3, P)
        cursor[0] = R0
        w1 = take(2, 32, P)
        cmpbuf = [take(32 + NBLK * KVC) for _ in range(2)]
        cpbuf = QT.rearrange("p a b -> p (a b)")[:, 0:32 + 4 * 2 * KVC]
        pos = take(2, 32)
        w2 = take(2, HD)
        ptmp = take(2, 2, P)
        pbias = take(4)
        chid = take(2, P)
        ce = take(2, P)
        pagesI = base0[0:1, cursor[0]:cursor[0] + P].bitcast(I32)
        cursor[0] += P
        top_cmp = cursor[0]
        phase()
        pagesA = base0[0:1, cursor[0]:cursor[0] + P].bitcast(I32)
        cursor[0] += P
        ohs = take(WIN + TSN + NBLK)
        RB = take(P)
        rel4 = take(NH)
        lastb = take(1)
        ownt = take(4)
        maskn = take(PAIRS, TSN)
        maskw = take(4)
        rowt = take(PAIRS, P, parts=TSN)
        rowh = take(NH)
        rowkv = take(4)
        samekv = take(P)
        earlier = take(NSB, NSB)
        b31 = take(1)
        gateS = take(PAIRS, 3)
        Qbd = take(NB, 2, 2, G, TS)
        gateP = take(3, GC)
        att0 = cursor[0]
        ohtoe = take(TOE, parts=NBK + 1)
        rel33 = take(NH, parts=NBK + 1)
        ohcp = take(8, P, parts=NBK)
        maskc = take(2, 4)
        biasc = take(2, 4, NH)
        wgate = take(KD, GC)
        sq3 = take(KD, T)
        toe = take(TOE, parts=NH)
        Tb = take(NH, 2 * P)
        Tflip = take(NH, 2 * P)
        flip = take(P)
        qst = take(2, TP)
        Sp = take(2, 2, 2 * P)
        Sc = take(2, 4)
        mp = take(2, 3)
        sp = take(2, 3)
        PTp = take(2, 4, P)
        PTc = take(2, P, parts=4)
        top_pa = cursor[0]
        cursor[0] = att0
        Sx = take(PAST + TSN + WIN + TSN)
        PT = take(20, P)
        PTn = take(3, P, parts=TSN)
        KTs = QT.rearrange("p a b -> p (a b)")[:, 0:2048].rearrange("p (a b c) -> p a b c", a=2, b=2)
        Kr = take(5, 4, KVC)
        V = take(2, 20, KVC)
        Qst = take(2, 2, 32)
        kcs = take(2, 2, NBLK)
        vcs = take(2, KVC, parts=NBLK)
        Scs = take(NBLK)
        Pcs = take(NBLK)
        score = take(NSB)
        rank = take(NSB)
        selb = take(NSB)
        sm = take(8)
        Om = take(KVC)
        Od = take(2, HD)
        mnst = take(TSN)
        top_sa = cursor[0]
        cmpA = view(att0, NSB, NSB)
        cmpB = view(att0 + NSB * NSB, NSB, NSB)
        phase()
        Xn = take(3, D)
        XeT = take(KD, P)
        He = take(FC, P)
        Ye = take(D)
        ee = take(2, 2, P)
        Se = take(3, P)
        SwT = take(T)
        posb = take(NE, T)
        cwb = take(NE, T)
        wr = take(KD, NE)
        lg = take(3, NE)
        pe8 = take(3, NE)
        rk8 = take(3, NE)
        m8 = take(3, 8)
        mk8 = take(3, NE)
        comb = take(3, NE)
        pfx = take(3, NE)
        posm = take(3, 25)
        iotar = take(P)
        iotac = take(3)
        before = take(P)
        earl8 = take(64)
        roff = take(25)
        diag = take(NE, P)
        c3 = take(64)
        flag = base0[:, cursor[0]:cursor[0] + 1].bitcast(I32)
        flagf = base0[:, cursor[0] + 1:cursor[0] + 2]
        cursor[0] += 2
        sqM = view(cursor[0], KD, T)
        yout = view(cursor[0] + KD * T, 3, D)
        top_moe = cursor[0] + KD * T + 3 * D
        sizes = dict(l0=top_l0, cmp=top_cmp, pa=top_pa, sa=top_sa, moe=top_moe)
        assert max(sizes.values()) * 4 <= ARENA, (sizes, ARENA // 4)

        ps = ctx.enter_context(nc.psum_tensor("ps", [P, 8, 512], F32))
        toe_dram = nc.dram_tensor("toe_scratch", [NH, TOE], F32, kind="Internal").ap()

        MIX0, MIX1, FFN0, FFN1, KVN, FIN, BPW1, BDW, LNG, LNB, BPW2 = 0, 8, 16, 24, 32, 40, 48, 64, 72, 80, 88
        NORM = [MIX0, FFN0, KVN, MIX1, FFN1, FIN]
        TAP = 96

        plan = []

        def cols(w, c0, slot, n=256):
            return [(slot[:, 0:KD * n].rearrange("p (k n) -> p k n", k=KD),
                     w[:, c0:c0 + n].rearrange("(k p) n -> p k n", p=P))]

        def rows2(w, k):
            return lambda slot: [(slot.rearrange("p (k n) -> p k n", k=2),
                                  w[k * 2 * P:(k + 1) * 2 * P, :].rearrange("(k p) n -> p k n", p=P))]

        for j in range(4):
            for half in range(2):
                plan.append(lambda s, c=half * D + j * 256: cols(a["conv_w_pw1"][0], c, s))
        for j in range(4):
            plan.append(lambda s, c=j * 256: cols(a["conv_w_pw2"][0], c, s))
        for u in range(11):
            for w in ("ffn_w_gate", "ffn_w_up"):
                plan.append(lambda s, w=w, c=u * 256: cols(a[w][0], c, s))
        for k in range(11):
            plan.append(rows2(a["ffn_w_down"][0], k))
        for j in range(6):
            plan.append(lambda s, c=j * 256: cols(a["w_kv"], c, s))

        def win_slot(s, pr, gg):
            w = a["nsa_w_in"][0]
            v = s.rearrange("p (k g q d) -> p k g q d", k=KD, g=2, q=2)
            return [(v[:, :, g2, q, :], w[:, c0:c0 + HD].rearrange("(k p) n -> p k n", p=P))
                    for q in range(2) for g2 in range(2)
                    for c0 in [512 * pr + 256 * q + HD * (2 * gg + g2)]]
        for pr in range(2):
            for gg in range(2):
                plan.append(lambda s, pr=pr, gg=gg: win_slot(s, pr, gg))

        def wout_slot(s, c0):
            w = a["nsa_w_out"][0][:, c0:c0 + 256].rearrange("(p q g d) n -> p q d g n", p=2, q=2, g=4)
            v = s.rearrange("x (p g n) -> x p g n", p=2, g=4)
            return [(v[64 * q:64 * q + 64, pr], w[pr, q]) for pr in range(2) for q in range(2)]
        for j in range(4):
            plan.append(lambda s, c=j * 256: wout_slot(s, c))
        NPRE = len(plan)
        full = [sem(f"ring_full{s}") for s in range(RING)]
        counts, need = [0] * RING, []
        for g, f in enumerate(plan):
            s = g % RING
            counts[s] += 16 * len(f(ring[:, s, :]))
            need.append((s, counts[s]))
        per = [len(range(s, 33, RING)) for s in range(RING)]
        M0 = -(-NPRE // RING) * RING
        START = dict(pw1=0, pw2=8, ffn=12, down=34, kv=45, win=51, wout=55)
        assert START["wout"] + 4 == NPRE

        slot_used = sem("slot_used")

        class Link:

            def __init__(self, eng, name):
                self.eng, self.sem, self.n, self.off = eng, sem(name), 0, None

            def __call__(self, ins):
                self.n += 1
                ins.then_inc(self.sem, 1)
                self.eng.wait_ge(self.sem, self.n if self.off is None else self.off + self.n)
                return ins

            def loop(self, i, per_turn):
                self.start, self.per, self.off = self.n, per_turn, i * per_turn

            def end(self, turns):
                assert self.n - self.start == self.per, (self.n - self.start, self.per)
                self.n, self.off = self.start + self.per * turns, None

        class Dyn:

            def __init__(self, i, per):
                self.i, self.per = i, per

            def __call__(self, n):
                return self.i * self.per + n

        block = ctx.enter_context(nc.Block())

        @block.sync
        def _(sp):
            for g, f in enumerate(plan):
                if g >= RING:
                    sp.wait_ge(slot_used, g - RING + 1)
                s = g % RING
                for dst, src in f(ring[:, s, :]):
                    sp.dma_start(dst, src).then_inc(full[s], 16)

            def experts(e, turn):
                for k in range(33):
                    sp.wait_ge(slot_used, turn * EPAD + (M0 + k - RING + 1))
                    slot = ring[:, k % RING, :]
                    if k < 22:
                        w = a["moe_w_up" if k % 2 else "moe_w_gate"][0]
                        c0 = (k // 2) * 256
                        src = w[bass.ds(e, 1), :, c0:c0 + 256].rearrange("e (k p) n -> p (e k) n", p=P)
                        dst = slot.rearrange("p (k n) -> p k n", k=KD)
                    else:
                        r0 = (k - 22) * 2 * P
                        src = a["moe_w_down"][0][bass.ds(e, 1), r0:r0 + 2 * P, :].rearrange(
                            "e (k p) n -> p (e k) n", p=P)
                        dst = slot.rearrange("p (k n) -> p k n", k=2)
                    sp.dma_start(dst, src).then_inc(full[k % RING], 16)

            with sp.Fori(0, NE, 1) as e:
                experts(e, e)
            sp.wait_ge(sem("flag_ready"), 1)
            over = sp.value_load(flag[0:1, 0:1], min_val=0, max_val=1)
            with sp.If(over):
                with sp.Fori(1, 3, 1) as r:
                    with sp.Fori(0, NE, 1) as e:
                        experts(e, r * NE + e)
            for t, (t0, n) in enumerate(TILES):
                sp.wait_ge(sem("y_ready"), t + 1)
                dst = out["y_prompt"][0, t0:t0 + n] if t < 2 else out["y_sample"].rearrange("b t d -> (b t) d")
                sp.dma_start(dst, yout[0:n, t, :]).then_inc(sem("y_stored"), 16)
            sp.wait_ge(sem("y_stored"), 48)

        @block.gpsimd
        def _(gp):
            nc.gpsimd.memset(gsc, 0.0).then_inc(sem("held_cmp"), 1)
            gp.wait_ge(sem("pw1_ev"), 4)
            nc.gpsimd.tensor_copy(tail.rearrange("p c (b r) -> p c b r", b=NB), fullS[:, :, :, TS:])\
              .then_inc(sem("tail_ready"), 1)
            gp.wait_ge(sem("convout_ready"), 3)
            gp.dma_start(out["conv_prompt"][0, 0], convo[0:30, 0, :]).then_inc(sem("stored"), 16)
            for j in range(2):
                gp.dma_start(out["conv_sample"][0, 4 * j:4 * j + 4].rearrange("b r d -> (b r) d"),
                             convo[0:120, 1 + j, :]).then_inc(sem("stored"), 16)
            gp.wait_ge(sem("stored"), 48)
            gp.wait_ge(sem("l0_done"), 1)
            gp.dma_start(pagesI, a["page_table"].rearrange("b n -> (b n)").unsqueeze(0)).then_inc(sem("pt_in"), 16)
            for kvi in range(2):
                src = a["cmp_w1"][kvi].rearrange("(l s d) h -> s l d h", s=2, d=32)
                srcp = a["cmp_pos"][kvi].rearrange("l (s d) -> s l d", s=2)
                for s in range(2):
                    gp.dma_start(w1[64 * s:64 * s + 64, kvi], src[s]).then_inc(sem("w1_in"), 16)
                    gp.dma_start(pos[64 * s:64 * s + 64, kvi], srcp[s]).then_inc(sem("w1_in"), 16)
                gp.dma_start(w2[:, kvi, :], a["cmp_w2"][kvi]).then_inc(sem("w1_in"), 16)
            gp.wait_ge(sem("pt_in"), 16)

            def hold(name, n):
                gp.wait_ge(sem(name), n + 1)
                nc.gpsimd.tensor_tensor(gsc[:, 0:1], gsc[:, 1:2], gsc[:, 2:3], ALU.add).then_inc(sem(name), 1)

            def pages_in(b, kvi, buf, in_sem):
                for n in range(NPG):
                    pg = gp.value_load(pagesI[0:1, bass.ds(b * NPG + n, 1)], min_val=0, max_val=NPHYS - 1)
                    src = a["cache_kv"][bass.ds(pg, 1), :, kvi].rearrange("g (b l) k d -> l (g b) (k d)", b=2)
                    for s in range(2):
                        off = 32 * (1 - s) + n * 2 * KVC
                        dst = cmpbuf[buf][64 * s:64 * s + 64, off:off + 2 * KVC].rearrange("p (b n) -> p b n", b=2)
                        gp.dma_start(dst, src).then_inc(in_sem, 16)

            with gp.Fori(0, NB, 1) as b:
                for kvi in range(2):
                    gp.wait_ge(sem("cmp_used"), b * 2 + (kvi + 1))
                    hold("held_cmp", b * 2 + kvi)
                    pages_in(b, kvi, kvi, sem(f"cmp_in{kvi}"))
            gp.wait_ge(sem("kvp_stored"), 32)
            srcp = out["kv_prompt"][0][:, 0:2].rearrange("(b l) s k d -> l b (s k d)", b=4)
            for s in range(2):
                off = 32 * (1 - s)
                gp.dma_start(cpbuf[64 * s:64 * s + 64, off:off + 4 * 2 * KVC].rearrange("p (b n) -> p b n", b=4),
                             srcp).then_inc(sem("cp_in"), 16)

            gp.wait_ge(sem("held_cmp"), 2 * NB + 1)
            gp.sem_inc(sem("held_att"), 1)
            gp.wait_ge(sem("cmp_done"), 1)
            gp.dma_start(pagesA, a["page_table"].rearrange("b n -> (b n)").unsqueeze(0)).then_inc(sem("pt2_in"), 16)
            gp.wait_ge(sem("pt2_in"), 16)
            gp.wait_ge(sem("prompt_done"), 1)
            swin = a["state_win_kv"]

            with gp.Fori(0, PAIRS, 1) as pr:
                gp.wait_ge(sem("o_mm"), pr + 1)
                hold("held_att", pr * 11)
                for kt in range(5):
                    for b2 in range(2):
                        u = kt * 2 + b2
                        slot = u % 5
                        gp.wait_ge(sem("kt_out"), pr * 10 + (u + 1))
                        hold("held_att", pr * 11 + (u + 1))
                        if kt < 4:
                            for n in range(4):
                                pg = gp.value_load(pagesA[0:1, bass.ds(pr * 32 + (b2 * NPG + kt * 4 + n), 1)],
                                                   min_val=0, max_val=NPHYS - 1)
                                ck = a["cache_kv"][bass.ds(pg, 1), :, 2].rearrange("g l k d -> (g l) (k d)")
                                cv = a["cache_kv"][bass.ds(pg, 1), :, 3].rearrange("g l k d -> (g l) (k d)")
                                gp.dma_start(Kr[:, slot, n, :], ck).then_inc(sem(f"k_in{slot}"), 16)
                                gp.dma_start(V[:, b2, kt * 4 + n, :], cv).then_inc(sem("v_in"), 16)
                        else:
                            w = swin[bass.ds(pr * 2 + b2, 1)].rearrange("o (n l) s k d -> l (o n) s (k d)", l=P)
                            gp.dma_start(Kr[:, slot, :, :], w[:, :, 0, :]).then_inc(sem(f"k_in{slot}"), 64)
                            gp.dma_start(V[:, b2, 16:20, :], w[:, :, 1, :]).then_inc(sem("v_in"), 64)
            gp.wait_ge(sem("stored"), 48)

        @block.scalar
        def _(act):
            sc = nc.scalar
            link = Link(act, "act_chain")
            act.dma_start(ident, a["ident"]).then_inc(sem("in_ident"), 16)
            rows = [(a["norm_mix"], 0, 16), (a["norm_ffn"], 16, 16), (a["norm_kv"], 32, 8), (a["norm_final"], 40, 8),
                    (a["conv_b_pw1"], 48, 16), (a["conv_b_dw"], 64, 8), (a["conv_ln_g"], 72, 8),
                    (a["conv_ln_b"], 80, 8), (a["conv_b_pw2"], 88, 8)]
            for v, r0, n in rows:
                src = v.rearrange("(n p) -> n p", p=P) if len(v.shape) == 1 else v.rearrange("a (n p) -> (a n) p", p=P)
                act.dma_start(vrow[r0:r0 + n, 0, :], src).then_inc(sem("in_vec"), 16)
            wdw = a["conv_w_dw"][0].rearrange("w (n p) -> (w n) p", p=P)
            for j in range(2):
                act.dma_start(vrow[0:124, 1 + j, :], wdw[124 * j:124 * j + 124]).then_inc(sem("in_vec"), 16)
            for t, (t0, n) in enumerate(TILES):
                src = a["x_prompt"][0, t0:t0 + n] if t < 2 else a["x_sample"].rearrange("b t d -> (b t) d")
                act.dma_start(xnat[0:n, t, :], src).then_inc(sem("in_x"), 16)
            for j in range(2):
                act.dma_start(scn[:, j, :], a["state_conv"][0, 4 * j:4 * j + 4].rearrange("b r d -> (b r) d"))\
                   .then_inc(sem("in_x"), 16)
            act.dma_start(out["win_sample"][:, 0:WIN - TS].rearrange("b w s k d -> b (w s k d)"),
                          a["state_win_kv"][:, TS:WIN].rearrange("b w s k d -> b (w s k d)")).then_inc(sem("stored_a"), 16)

            def norm(n, bank=0):
                act.wait_ge(sem("norm_sum"), n + 1)
                sc.activation(rstd, ps[:, bank, 0:T], ACT.Sqrt, scale=1.0 / D, bias=eps).then_inc(sem("norm_root"), 1)

            norm(0)
            for u in range(4):
                act.wait_ge(slot_used, START["pw1"] + 2 * u + 2)
                if u >= 2:
                    act.wait_ge(sem("pw1_ev"), u - 1)
                bk = 4 * (u % 2)
                for c in range(2):
                    ins = sc.activation(e0[:, u % 2, c, :], ps[:, bk + 2 + c, 0:T], ACT.Exp, scale=-1.0,
                                        bias=nvec[:, 2 * u + c:2 * u + c + 1])
                ins.then_inc(sem("pw1_exp"), 1)
            for j in range(3):
                act.wait_ge(sem("convo_mm"), j + 1)
                n = 30 if j == 0 else 120
                sc.activation(convo[0:n, j, :], ps[0:n, 2 * j:2 * j + 2, :].rearrange("p a b -> p (a b)"), ACT.Copy)\
                  .then_inc(sem("convout_ready"), 1)
            act.wait_ge(sem("ln_sum"), 1)
            sc.activation(rstd, ps[:, 6, 0:T], ACT.Copy, scale=1.0 / D).then_inc(sem("ln_mean"), 1)
            act.wait_ge(sem("ln_sum"), 2)
            act.wait_ge(sem("ln_centred"), 1)
            sc.activation(rstd, ps[:, 7, 0:T], ACT.Sqrt, scale=1.0 / D, bias=eps).then_inc(sem("ln_root"), 1)
            act.wait_ge(sem("ln_hat"), 1)
            for c in range(KD):
                sc.activation(sqL0[:, c, :], acc[:, c, :], ACT.Exp, scale=nvec[:, 8 + c:9 + c],
                              bias=nvec[:, 16 + c:17 + c]).then_inc(sem("ln_exp"), 1)
            norm(1)
            for u in range(11):
                act.wait_ge(slot_used, START["ffn"] + 2 * u + 2)
                if u >= 2:
                    act.wait_ge(sem("ffn_ev"), u - 1)
                bk = 4 * (u % 2)
                sc.activation(e0[:, u % 2], ps[:, bk:bk + 2, 0:T], ACT.Exp, scale=-1.0).then_inc(sem("ffn_exp"), 1)
            norm(2)
            for j in range(6):
                act.wait_ge(slot_used, START["kv"] + j + 1)
                bk = 4 * (j % 2)
                sc.activation(kv[:, 0:2, j * KVC:(j + 1) * KVC], ps[:, bk:bk + 2, 0:KVC], ACT.Copy)
                sc.activation(kv[0:TSN, 2, j * KVC:(j + 1) * KVC], ps[0:TSN, bk + 2, 0:KVC], ACT.Copy)\
                  .then_inc(sem("kv_ev"), 1)
            act.wait_ge(sem("kv_ev"), 6)
            for t in range(2):
                act.dma_start(out["kv_prompt"][0, t * P:(t + 1) * P].rearrange("t s k d -> t (s k d)"),
                              kv[:, t, 0:4 * KVC]).then_inc(sem("kvp_stored"), 16)
                act.dma_start(out["win_prompt"][0, t * P:(t + 1) * P].rearrange("t s k d -> t (s k d)"),
                              kv[:, t, 4 * KVC:]).then_inc(sem("stored_a"), 16)
            act.dma_start(out["kv_sample"].rearrange("b t s k d -> (b t) (s k d)"), kv[0:TSN, 2, 0:4 * KVC])\
               .then_inc(sem("stored_a"), 16)
            act.dma_start(out["win_sample"][:, WIN - TS:].rearrange("b t s k d -> b t (s k d)"),
                          kv[0:TSN, 2, 4 * KVC:]).then_inc(sem("stored_a"), 16)
            with act.Fori(0, NB, 1) as b:
                for kvi in range(2):
                    act.wait_ge(sem("cmp_used"), b * 2 + (kvi + 3))
                    sc.activation(ce[:, kvi, :], ps[:, kvi, 0:P], ACT.Exp, scale=-1.0,
                                  bias=pbias[:, 2 + kvi:3 + kvi]).then_inc(sem("ch_exp"), 1)
            for kvi in range(2):
                act.wait_ge(sem("cmp_used"), 2 * NB + kvi + 3)
                sc.activation(ce[:, kvi, 0:16], ps[:, kvi, 0:16], ACT.Exp, scale=-1.0,
                              bias=pbias[:, 2 + kvi:3 + kvi]).then_inc(sem("ch_exp"), 1)
            act.wait_ge(sem("cmp_done"), 1)
            for s in range(2):
                act.wait_ge(sem("kt_mm"), s + 1)
                sc.activation(KT[:, s], ps[:, 4 + 2 * s:6 + 2 * s, 0:T], ACT.Copy).then_inc(sem("kt_ev"), 1)
            for dst, name in [(ohs, "oh_smp"), (lastb, "last_bucket"), (ownt, "own_token"), (maskw, "mask_win"),
                              (rowh, "row_head"), (rowkv, "row_kv"), (samekv, "same_kv"), (flip, "flip"), (ohtoe, "oh_toe"),
                              (rel33[0:NBK, :], "rel_bias")]:
                act.dma_start(dst, a[name]).then_inc(sem("in_att"), 16)
            for dst, name in [(maskn, "mask_new"), (rowt, "row_token"), (earlier, "earlier"), (ohcp, "oh_cmp_p"),
                              (maskc, "mask_cmp_p")]:
                act.dma_start(dst, a[name].rearrange("p (a b) -> p a b", a=dst.shape[1])).then_inc(sem("in_att"), 16)
            for t in range(4):
                act.dma_start(rel4[32 * t:32 * t + 32, :], a["rel_bias"]).then_inc(sem("in_att"), 16)
            act.dma_start(wgate, a["nsa_w_in"][0][:, D:D + GC].rearrange("(k p) n -> p k n", p=P))\
               .then_inc(sem("in_att"), 16)
            norm(3)
            for j in range(4):
                act.wait_ge(slot_used, START["win"] + j + 1)
                bk = 2 * (j % 4)
                sc.activation(QT[:, 2 * j:2 * j + 2, :], ps[:, bk:bk + 2, 0:T], ACT.Copy, scale=HD ** -0.5)\
                  .then_inc(sem("q_ev"), 1)
            act.wait_ge(sem("gate_mm"), 1)
            sc.activation(gateP[:, 0:2, :], ps[:, 0:2, 0:GC], ACT.Exp, scale=-1.0)
            sc.activation(gateP[0:TSN, 2, :], ps[0:TSN, 2, 0:GC], ACT.Exp, scale=-1.0).then_inc(sem("gate_exp"), 1)
            act.wait_ge(sem("toe_mm"), 1)
            sc.activation(toe, ps[0:NH, 3, 0:TOE], ACT.Copy).then_inc(sem("toe_ev"), 1)
            act.wait_ge(sem("toe_ev"), 1)
            act.dma_start(toe_dram, toe).then_inc(sem("toe_out"), 16)
            act.wait_ge(sem("toe_out"), 16)
            skew = bass.AP(tensor=toe_dram.tensor, offset=0, ap=[[1, P], [TOE, NH], [1, 2 * P]])
            act.dma_start(Tflip, skew).then_inc(sem("toe_in"), 16)

            with act.Fori(0, G, 1) as g:
                for u in range(8):
                    w, qt = u % 2, u % 2
                    nk = P * (qt + 1)
                    n = g * 8 + (u + 1)
                    act.wait_ge(sem("pa_max"), n)
                    for br in range(2):
                        sc.activation(Sp[:, w, br, 0:nk], Sp[:, w, br, 0:nk], ACT.Exp, bias=mp[:, w, br:br + 1],
                                      accum_out=sp[:, w, br:br + 1])
                    sc.activation(Sc[:, w, :], Sc[:, w, :], ACT.Exp, bias=mp[:, w, 2:3]).then_inc(sem("pa_exp"), 1)
                    act.wait_ge(sem("pa_tr"), n)
                    sc.activation(PTc[:, w, :], ps[0:4, 4 + w, 0:P], ACT.Copy)
                    sc.activation(PTp[:, w, 0:2 * (qt + 1), :], ps[:, 2 + w, 0:2 * nk], ACT.Copy)\
                      .then_inc(sem("pa_pt"), 1)

            act.sem_inc(sem("kt_out"), 5)
            with act.Fori(0, PAIRS, 1) as pr:
                act.wait_ge(sem("sc_max"), pr + 1)
                sc.activation(Scs, Scs, ACT.Exp, bias=sm[:, 0:1], accum_out=sm[:, 1:2]).then_inc(sem("sc_exp"), 1)
                for u in range(10):
                    act.wait_ge(sem("kt_tr"), pr * 10 + (u + 1))
                    act.wait_ge(sem("s_unit"), pr * 10 + max(u, 1))
                    bk = 2 * (u % 2)
                    sc.activation(KTs[:, u % 2], ps[:, bk:bk + 2, :], ACT.Copy).then_inc(sem("kt_out"), 1)
                act.wait_ge(sem("s_max"), pr + 1)
                sc.activation(Sx[:, 0:PAST + TSN], Sx[:, 0:PAST + TSN], ACT.Exp, bias=sm[:, 2:3], accum_out=sm[:, 3:4])
                sc.activation(Sx[:, PAST + TSN:], Sx[:, PAST + TSN:], ACT.Exp, bias=sm[:, 4:5], accum_out=sm[:, 5:6])\
                  .then_inc(sem("s_exp"), 1)
                for c in range(5):
                    act.wait_ge(sem("pt_tr"), pr * 6 + (c + 1))
                    sc.activation(PT[:, 4 * c:4 * c + 4, :], ps[:, c % 4, :].rearrange("p (a b) -> p a b", a=4), ACT.Copy)\
                      .then_inc(sem("pt_out"), 1)
                act.wait_ge(sem("pt_tr"), pr * 6 + 6)
                sc.activation(PTn, ps[0:TSN, 4, 0:3 * P].rearrange("p (a b) -> p a b", a=3), ACT.Copy)\
                  .then_inc(sem("pt_out"), 1)
            act.wait_ge(sem("wout_done"), 1)
            for dst, name in [(iotar, "iota_row"), (iotac, "iota_col"), (before, "before"), (earl8, "earlier8"),
                              (roff, "round_off")]:
                act.dma_start(dst, a[name]).then_inc(sem("in_moe"), 16)
            act.dma_start(wr, a["moe_w_router"][0].rearrange("(k p) n -> p k n", p=P)).then_inc(sem("in_moe"), 16)
            norm(4)
            for t, (t0, n) in enumerate(TILES):
                act.wait_ge(sem("xr_mm"), t + 1)
                bk = 2 * (t % 2)
                sc.activation(Xn[0:n, t, :], ps[0:n, bk:bk + 2, :].rearrange("p a b -> p (a b)"), ACT.Copy)\
                  .then_inc(sem("xr_ev"), 1)
            act.wait_ge(sem("rt_max"), 1)
            for t, (t0, n) in enumerate(TILES):
                ins = sc.activation(pe8[0:n, t, :], lg[0:n, t, :], ACT.Exp, bias=m8[0:n, t, 0:1])
            ins.then_inc(sem("rt_exp"), 1)

            act.wait_ge(sem("xe_mm"), 1)
            sc.activation(XeT, ps[:, 0:2, :].rearrange("p a (b c) -> p (a b) c", c=P), ACT.Copy).then_inc(sem("xe_ev"), 1)

            def experts(turn):
                for u in range(11):
                    v = turn * 11 + u
                    act.wait_ge(slot_used, turn * EPAD + (M0 + 2 * u + 2))
                    act.wait_ge(sem("gu_ev"), v + 1)
                    sc.activation(ee[:, u % 2], ps[:, 2 + u % 2, 0:2 * P], ACT.Exp, scale=-1.0).then_inc(sem("gu_exp"), 1)
                act.wait_ge(slot_used, turn * EPAD + (M0 + 33))
                sc.activation(Ye, ps[:, 4:6, :].rearrange("p a b -> p (a b)"), ACT.Copy).then_inc(sem("y_ev"), 1)
                act.wait_ge(sem("xe_mm"), turn + 2)
                sc.activation(XeT, ps[:, 0:2, :].rearrange("p a (b c) -> p (a b) c", c=P), ACT.Copy)\
                  .then_inc(sem("xe_ev"), 1)

            with act.Fori(0, NE, 1) as e:
                experts(e)
            act.wait_ge(sem("flag_ready"), 1)
            over = act.value_load(flag[0:1, 0:1], min_val=0, max_val=1)
            with act.If(over):
                with act.Fori(1, 3, 1) as r:
                    with act.Fori(0, NE, 1) as e:
                        experts(r * NE + e)
            norm(5, 4)
            for t, (t0, n) in enumerate(TILES):
                act.wait_ge(sem("yo_mm"), t + 1)
                bk = 2 + 2 * t
                sc.activation(yout[0:n, t, :], ps[0:n, bk:bk + 2, :].rearrange("p a b -> p (a b)"), ACT.Copy)\
                  .then_inc(sem("y_ready"), 1)
            act.wait_ge(sem("stored_a"), 5 * 16)
            act.wait_ge(sem("kvp_stored"), 2 * 16)

        @block.vector
        def _(dve):
            v = nc.vector
            link = Link(dve, "dve_chain")
            link(v.memset(eps, EPS))
            v.memset(ones, 1.0).then_inc(sem("ones"), 1)
            v.memset(fullP[:, :, 0:CW - 1], 0.0)
            dve.wait_ge(sem("vec_mm"), 1)
            v.tensor_copy(vec[:, 0:96], ps[:, 0, 0:96])
            v.tensor_copy(vec[:, 96:96 + 124], ps[:, 0, 128:252])
            link(v.tensor_copy(vec[:, 96 + 124:], ps[:, 0, 256:380]))
            v.tensor_scalar(nvec[:, 0:8], vec[:, BPW1 + 8:BPW1 + 16], -1.0, None, ALU.mult)
            v.tensor_scalar(nvec[:, 8:16], vec[:, LNG:LNG + 8], -1.0, None, ALU.mult)
            v.tensor_scalar(nvec[:, 16:24], vec[:, LNB:LNB + 8], -1.0, None, ALU.mult).then_inc(sem("vec_ready"), 1)
            for c in range(KD):
                dve.wait_ge(sem("x_mm"), c + 1)
                v.tensor_copy(fullS[:, c, :, 0:CW - 1].rearrange("p (a b) r -> p a b r", a=2),
                              ps[:, 5 + c % 2, 0:240].rearrange("p (a b r) -> p a b r", a=2, b=4))
                link(v.tensor_copy(hT[:, c, :], ps[:, 1 + c % 4, 0:T]))
                v.tensor_tensor(acc[:, c, :], hT[:, c, :], hT[:, c, :], ALU.mult)\
                 .then_inc(sem("x_ev"), 1)
            v.memset(small[:, 0:1], 0.0).then_inc(sem("norm_sq"), 1)

            def norm_tail(n):
                dve.wait_ge(sem("norm_root"), n + 1)
                link(v.reciprocal(rstd, rstd))
                for c in range(KD):
                    col = NORM[n] + c
                    ins = v.scalar_tensor_tensor(out=xnT[:, c, :], in0=hT[:, c, :], scalar=vec[:, col:col + 1],
                                                 in1=rstd, op0=ALU.mult, op1=ALU.mult)
                ins.then_inc(sem("norm_out"), 1)

            def norm(n, sq):
                v.tensor_tensor(sq, hT, hT, ALU.mult).then_inc(sem("norm_sq"), 1)
                norm_tail(n)

            norm_tail(0)
            for u in range(4):
                dve.wait_ge(sem("pw1_exp"), u + 1)
                e = e0[:, u % 2]
                link(v.tensor_scalar_add(e, e, 1.0))
                link(v.reciprocal(e, e))
                for c in range(2):
                    cc = 2 * u + c
                    bk = 4 * (u % 2) + c
                    b = vec[:, BPW1 + cc:BPW1 + cc + 1]
                    v.scalar_tensor_tensor(out=fullP[:, cc, CW - 1:], in0=ps[:, bk, 0:TP], scalar=b,
                                           in1=e[:, c, 0:TP], op0=ALU.add, op1=ALU.mult)
                    ins = v.scalar_tensor_tensor(out=fullS[:, cc, :, CW - 1:],
                                                 in0=ps[:, bk, TP:T].rearrange("p (b t) -> p b t", b=NB), scalar=b,
                                                 in1=e[:, c, TP:T].rearrange("p (b t) -> p b t", b=NB),
                                                 op0=ALU.add, op1=ALU.mult)
                ins.then_inc(sem("pw1_ev"), 1)
            dve.wait_ge(sem("pw1_ev"), 4)
            taps = Link(dve, "tap_chain")
            fP, fS = fullP, fullS
            with dve.Fori(0, KD, 1) as c:
                base = c * (2 * CW)
                aP = acc[:, bass.ds(c, 1), 0:TP]
                aS = acc[:, bass.ds(c, 1), TP:T].rearrange("p o (b t) -> p (o b) t", b=NB)
                for w in range(CW):
                    tap = vec[:, bass.ds(c + (TAP + 8 * w), 1)]
                    for k, (o, f) in enumerate([(aP, fP[:, bass.ds(c, 1), w:w + TP]),
                                                (aS, fS[:, bass.ds(c, 1), :, w:w + TS].rearrange("p o b t -> p (o b) t"))]):
                        if w == 0:
                            ins = v.tensor_scalar(o, f, tap, vec[:, bass.ds(c + BDW, 1)], ALU.mult, ALU.add)
                        else:
                            dve.wait_ge(taps.sem, base + 2 * (w - 1) + k + 1)
                            ins = v.scalar_tensor_tensor(out=o, in0=f, scalar=tap, in1=o, op0=ALU.mult, op1=ALU.add)
                        ins.then_inc(taps.sem, 1)
            dve.wait_ge(taps.sem, KD * 2 * CW)
            v.memset(small[:, 1:2], 0.0).then_inc(sem("conv_done"), 1)
            dve.wait_ge(sem("ln_mean"), 1)
            link(v.tensor_tensor(acc, acc, rstd.unsqueeze(1).to_broadcast([P, KD, T]), ALU.subtract))
            v.tensor_tensor(sqL0, acc, acc, ALU.mult).then_inc(sem("ln_centred"), 1)
            dve.wait_ge(sem("ln_root"), 1)
            link(v.reciprocal(rstd, rstd))
            v.tensor_tensor(acc, acc, rstd.unsqueeze(1).to_broadcast([P, KD, T]), ALU.mult).then_inc(sem("ln_hat"), 1)
            for c in range(KD):
                dve.wait_ge(sem("ln_exp"), c + 1)
                e = sqL0[:, c, :]
                link(v.tensor_scalar_add(e, e, 1.0))
                link(v.reciprocal(e, e))
                link(v.tensor_scalar(acc[:, c, :], acc[:, c, :], vec[:, LNG + c:LNG + c + 1],
                                     vec[:, LNB + c:LNB + c + 1], ALU.mult, ALU.add))
                ins = v.tensor_tensor(xnT[:, c, :], acc[:, c, :], e, ALU.mult)
            ins.then_inc(sem("swish_ready"), 1)
            for j in range(4):
                dve.wait_ge(slot_used, START["pw2"] + j + 1)
                for c in range(2):
                    cc = 2 * j + c
                    ins = v.scalar_tensor_tensor(out=hT[:, cc, :], in0=ps[:, 2 * j + c, 0:T],
                                                 scalar=vec[:, BPW2 + cc:BPW2 + cc + 1], in1=hT[:, cc, :],
                                                 op0=ALU.add, op1=ALU.add)
                link(ins)
            norm(1, acc)
            for u in range(11):
                dve.wait_ge(sem("ffn_exp"), u + 1)
                e, bk = e0[:, u % 2], 4 * (u % 2)
                link(v.tensor_scalar_add(e, e, 1.0))
                link(v.reciprocal(e, e))
                link(v.tensor_tensor(e, e, ps[:, bk:bk + 2, 0:T], ALU.mult))
                if u == 0:
                    dve.wait_ge(sem("stored"), 48)
                v.tensor_tensor(Hf[:, 2 * u:2 * u + 2, :], e, ps[:, bk + 2:bk + 4, 0:T], ALU.mult)\
                 .then_inc(sem("ffn_ev"), 1)
            dve.wait_ge(slot_used, START["down"] + 11)
            link(v.tensor_tensor(hT, hT, ps[:, :, 0:T], ALU.add))
            norm(2, acc)
            v.memset(small[:, 2:3], 0.0).then_inc(sem("l0_done"), 1)
            dve.wait_ge(sem("w1_in"), 160)
            pt = QT.rearrange("p a b -> p (a b)")[:, 0:16 * P].rearrange("p (a b) -> p a b", a=16)
            for kvi in range(2):
                for j in range(2):
                    link(v.tensor_tensor(pt, w1[:, kvi, 16 * j:16 * j + 16],
                                         pos[:, kvi, 16 * j:16 * j + 16].unsqueeze(2).to_broadcast([P, 16, P]), ALU.mult))
                    ins = v.tensor_reduce(ptmp[:, kvi, j, :], pt.rearrange("p a b -> p b a"), AXX, ALU.add)
                    ins.then_inc(sem("pos_red"), 1)
                    dve.wait_ge(sem("pos_red"), 2 * kvi + j + 1)
            dve.wait_ge(sem("pos_mm"), 2)
            v.tensor_copy(pbias[:, 0:2], ps[:, 3, 0:2])
            v.tensor_scalar(pbias[:, 2:4], ps[:, 3, 0:2], -1.0, None, ALU.mult).then_inc(sem("pb_ready"), 1)
            dve.wait_ge(sem("pb_ready"), 1)

            def compress(n, kvi, ncol, dstk, dstv, rows):
                dve.wait_ge(sem("ch_exp"), n + 1)
                e, h = ce[:, kvi, 0:ncol], chid[:, kvi, 0:ncol]
                link(v.tensor_scalar_add(e, e, 1.0))
                link(v.reciprocal(e, e))
                v.scalar_tensor_tensor(out=h, in0=ps[:, kvi, 0:ncol], scalar=pbias[:, kvi:kvi + 1], in1=e,
                                       op0=ALU.add, op1=ALU.mult).then_inc(sem("ch_ready"), 1)
                dve.wait_ge(sem("co_mm"), n + 1)
                if kvi == 0:
                    v.tensor_copy(dstk, ps[:, 4, 0:2 * rows].rearrange("p (a o b) -> p a o b", a=2, o=1))\
                     .then_inc(sem("co_ev"), 1)
                else:
                    v.tensor_copy(dstv, ps[0:rows, 5, 0:KVC].unsqueeze(1)).then_inc(sem("co_ev"), 1)
            with dve.Fori(0, NB, 1) as b:
                link.loop(b, 4)
                for kvi in range(2):
                    compress(b * 2 + kvi, kvi, P, kcT[:, :, bass.ds(b, 1), :], vc[:, bass.ds(b, 1), :], NBLK)
                link.end(NB)
            for kvi in range(2):
                compress(2 * NB + kvi, kvi, 16, kcTp.unsqueeze(2), vcp.unsqueeze(1), 4)
            dve.wait_ge(sem("co_ev"), 2 * NB + 2)
            v.memset(small[:, 3:4], 0.0).then_inc(sem("cmp_done"), 1)
            norm(3, sq3)
            dve.wait_ge(sem("in_att"), 20 * 16)
            v.memset(rel33[NBK:NBK + 1, :], NEG)
            v.tensor_tensor(RB.rearrange("p (b h t) -> p b h t", b=2, h=NH),
                            rel4.unsqueeze(1).unsqueeze(3).to_broadcast([P, 2, NH, 4]),
                            ownt.unsqueeze(1).unsqueeze(1).to_broadcast([P, 2, NH, 4]), ALU.mult)\
             .then_inc(sem("rb_ready"), 1)
            v.memset(Qbd, 0.0)
            dve.wait_ge(sem("gate_exp"), 1)
            link(v.tensor_scalar_add(gateP[:, 0:2, :], gateP[:, 0:2, :], 1.0))
            link(v.reciprocal(gateP[:, 0:2, :], gateP[:, 0:2, :]))
            link(v.tensor_scalar_add(gateP[0:TSN, 2, :], gateP[0:TSN, 2, :], 1.0))
            v.reciprocal(gateP[0:TSN, 2, :], gateP[0:TSN, 2, :]).then_inc(sem("gate_ready"), 1)
            dve.wait_ge(sem("q_ev"), 4)
            qv = QT[:, :, TP:T].rearrange("p (a g) (b t) -> p a g b t", a=2, b=NB)
            for q in range(2):
                for pr in range(2):
                    s = slice(64 * q, 64 * q + 64)
                    for b in range(2):
                        v.tensor_copy(Qbd[s, 4 * b:4 * b + 4, pr, q],
                                      qv[s, pr, :, 4 * b:4 * b + 4].rearrange("p g b t -> p b g t"))
            dve.wait_ge(sem("bias_mm"), 1)
            v.tensor_copy(b31, ps[:, 5, 0:1])
            mneg = small[:, 8:16].rearrange("p (a b) -> p a b", a=2)
            link(v.tensor_scalar(mneg, maskc, -1.0, -NEG, ALU.add, ALU.mult))
            link(v.tensor_tensor(biasc, ps[:, 4, 0:8 * NH].rearrange("p (a b c) -> p a b c", a=2, b=4),
                                 mneg.unsqueeze(3).to_broadcast([P, 2, 4, NH]), ALU.add))
            for pr in range(PAIRS):
                dve.wait_ge(sem("gs_mm"), PAIRS)
                tmp = small[:, 16:64].rearrange("p (h b) -> p h b", h=NH)
                link(v.tensor_tensor(tmp, ps[:, 6, pr * GC:(pr + 1) * GC].rearrange("p (h b) -> p h b", h=NH),
                                     rowh.unsqueeze(2).to_broadcast([P, NH, 3]), ALU.mult))
                link(v.tensor_reduce(gateS[:, pr, :], tmp.rearrange("p h b -> p b h"), AXX, ALU.add))
            v.memset(small[:, 0:1], 0.0).then_inc(sem("prep_done"), 1)
            dve.wait_ge(sem("flip_mm"), 1)
            link(v.tensor_copy(Tb.rearrange("p (a b) c -> p a (b c)", a=8), ps[:, :, :]))

            def unit(u):
                return (u // 4, (u // 2) % 2, u % 2)

            with dve.Fori(0, G, 1) as g:
                link.loop(g, 8 * 5 + 1)
                v.tensor_copy(qst[:, 0:1, :], QT[:, bass.ds(g, 1), 0:TP])
                v.tensor_copy(qst[:, 1:2, :], QT[:, bass.ds(g + 4, 1), 0:TP]).then_inc(sem("pa_q"), 1)

                def front(u):
                    pr, q, qt = unit(u)
                    nk, w = P * (qt + 1), u % 2
                    h = g + (8 * pr + 4 * q)
                    dve.wait_ge(sem("pa_qk"), g * 8 + (u + 1))
                    v.tensor_tensor(Sp[:, w, :, 0:nk], ps[:, w, 0:2 * nk].rearrange("p (a b) -> p a b", a=2),
                                    Tb[:, bass.ds(h, 1), 2 * P - nk:].to_broadcast([P, 2, nk]), ALU.add)
                    link(v.tensor_tensor(Sc[:, w, :], ps[:, 6 + w, 0:4],
                                         biasc[:, qt, :, bass.ds(h, 1)].rearrange("p a b -> p (a b)"), ALU.add))
                    v.tensor_reduce(mp[:, w, 0:2], Sp[:, w, :, 0:nk], AXX, ALU.max, negate=True)
                    v.tensor_reduce(mp[:, w, 2:3], Sc[:, w, :], AXX, ALU.max, negate=True).then_inc(sem("pa_max"), 1)

                def back(u):
                    pr, q, qt = unit(u)
                    nk, w = P * (qt + 1), u % 2
                    h3 = g * 3 + 3 * (8 * pr + 4 * q)
                    dve.wait_ge(sem("pa_exp"), g * 8 + (u + 1))
                    link(v.tensor_tensor(Sc[:, w, :], Sc[:, w, :], maskc[:, qt, :], ALU.mult))
                    link(v.tensor_reduce(sp[:, w, 2:3], Sc[:, w, :], AXX, ALU.add))
                    link(v.tensor_scalar(sp[:, w, :], sp[:, w, :], TINY, None, ALU.max))
                    link(v.reciprocal(sp[:, w, :], sp[:, w, :]))
                    gq = gateP[:, qt, :]
                    v.tensor_tensor(mp[:, w, 0:2], sp[:, w, 0:2], gq[:, bass.ds(h3 + 1, 2)], ALU.mult)
                    v.tensor_tensor(mp[:, w, 2:3], sp[:, w, 2:3], gq[:, bass.ds(h3, 1)], ALU.mult)\
                     .then_inc(sem("pa_fac"), 1)
                    dve.wait_ge(sem("pa_fac"), g * 8 + (u + 1))
                    v.tensor_tensor(Sp[:, w, :, 0:nk], Sp[:, w, :, 0:nk],
                                    mp[:, w, 0:2].unsqueeze(2).to_broadcast([P, 2, nk]), ALU.mult)
                    v.tensor_scalar(Sc[:, w, :], Sc[:, w, :], mp[:, w, 2:3], None, ALU.mult).then_inc(sem("pa_p"), 1)

                def done(u):
                    pr, q, qt = unit(u)
                    dve.wait_ge(sem("pa_pv"), g * 8 + (u + 1))
                    s = slice(64 * q, 64 * q + 64)
                    v.tensor_copy(OT[s, bass.ds(g + 4 * pr, 1), qt * P:qt * P + P],
                                  ps[s, 4 + u % 2, P:2 * P].unsqueeze(1)).then_inc(sem("pa_o"), 1)
                front(0)
                for u in range(8):
                    if u < 7:
                        if u >= 1:
                            dve.wait_ge(sem("pa_tr"), g * 8 + u)
                        front(u + 1)
                    back(u)
                    if u >= 1:
                        done(u - 1)
                done(7)
                link(v.memset(small[:, 4:5], 0.0))
                link.end(G)
            dve.wait_ge(sem("pa_o"), 8 * G + 1)
            v.memset(small[:, 5:6], 0.0).then_inc(sem("prompt_done"), 1)
            link(v.memset(score, FORCE))

            NS = PAST + TSN
            with dve.Fori(0, PAIRS, 1) as pr:
                link.loop(pr, 14)
                v.tensor_copy(Qst, Qbd.rearrange("p b a q g t -> p (b a) (q g t)")[:, bass.ds(pr * 4, 4), :]
                              .rearrange("p (b a) n -> p b a n", b=2))
                v.tensor_copy(kcs, kcT[:, :, bass.ds(pr * 2, 2), :])
                v.tensor_copy(mnst.unsqueeze(1), maskn[:, bass.ds(pr, 1), :])
                v.tensor_copy(vcs, vc[:, bass.ds(pr * 2, 2), :]).then_inc(sem("st_ready"), 1)
                dve.wait_ge(sem("sc_mm"), pr + 1)
                link(v.tensor_scalar(Scs, ps[:, 6, 0:NBLK], b31, None, ALU.add))
                v.tensor_reduce(sm[:, 0:1], Scs, AXX, ALU.max, negate=True).then_inc(sem("sc_max"), 1)
                dve.wait_ge(sem("sc_exp"), pr + 1)
                link(v.tensor_scalar(sm[:, 1:2], sm[:, 1:2], TINY, None, ALU.max))
                link(v.reciprocal(sm[:, 1:2], sm[:, 1:2]))
                v.tensor_scalar(Pcs, Scs, sm[:, 1:2], None, ALU.mult).then_inc(sem("pc_ready"), 1)
                dve.wait_ge(sem("pc_ready"), pr + 1)
                v.tensor_scalar(Scs, Pcs, gateS[:, bass.ds(pr, 1), 0:1].rearrange("p a b -> p (a b)"), None, ALU.mult)
                dve.wait_ge(sem("imp_mm"), pr + 1)
                link(v.tensor_copy(score[:, 1:NBLK - 1], ps[:, 6, 32 + 1:32 + NBLK - 1]))
                si = score.unsqueeze(2).to_broadcast([P, NSB, NSB])
                sj = score.unsqueeze(1).to_broadcast([P, NSB, NSB])
                v.tensor_tensor(cmpA, sj, si, ALU.is_gt)
                link(v.tensor_tensor(cmpB, sj, si, ALU.is_equal))
                link(v.tensor_tensor(cmpB, cmpB, earlier, ALU.mult))
                link(v.tensor_tensor(cmpA, cmpA, cmpB, ALU.add))
                link(v.tensor_reduce(rank, cmpA, AXX, ALU.add))
                link(v.tensor_scalar(selb, rank, float(TOPN), NEG, ALU.is_ge, ALU.mult))
                for kt in range(4):
                    dve.wait_ge(sem("s_unit"), pr * 10 + (2 * kt + 3))
                    bk = 4 + kt % 2
                    v.scalar_tensor_tensor(out=Sx[:, kt * 512:(kt + 1) * 512].rearrange("p (b l) -> p b l", b=8),
                                           in0=ps[:, bk, :].rearrange("p (b l) -> p b l", b=8), scalar=b31,
                                           in1=selb[:, 8 * kt:8 * kt + 8].unsqueeze(2).to_broadcast([P, 8, BLOCK]),
                                           op0=ALU.add, op1=ALU.add).then_inc(sem("s_ev"), 1)
                dve.wait_ge(sem("s_unit"), pr * 10 + 11)
                link(v.tensor_scalar(Sx[:, NS:NS + WIN], ps[:, 4, :], b31, None, ALU.add))
                v.tensor_tensor(Sx[:, NS:NS + 4], Sx[:, NS:NS + 4], maskw, ALU.add).then_inc(sem("s_ev"), 1)
                dve.wait_ge(sem("s_new"), pr + 1)
                for j, o in enumerate([PAST, NS + WIN]):
                    ins = v.scalar_tensor_tensor(out=Sx[:, o:o + TSN], in0=ps[:, 7, 32 * j:32 * j + 32], scalar=b31,
                                                 in1=mnst, op0=ALU.add, op1=ALU.add)
                link(ins)
                v.tensor_reduce(sm[:, 2:3], Sx[:, 0:NS], AXX, ALU.max, negate=True)
                v.tensor_reduce(sm[:, 4:5], Sx[:, NS:], AXX, ALU.max, negate=True).then_inc(sem("s_max"), 1)
                dve.wait_ge(sem("s_exp"), pr + 1)
                for j in range(2):
                    s = sm[:, 3 + 2 * j:4 + 2 * j]
                    ins = v.tensor_scalar(s, s, TINY, None, ALU.max)
                link(ins)
                for j in range(2):
                    s = sm[:, 3 + 2 * j:4 + 2 * j]
                    ins = v.reciprocal(s, s)
                link(ins)
                for j in range(2):
                    s = sm[:, 3 + 2 * j:4 + 2 * j]
                    ins = v.tensor_tensor(s, s, gateS[:, bass.ds(pr, 1), 1 + j:2 + j].rearrange("p a b -> p (a b)"),
                                          ALU.mult)
                ins.then_inc(sem("s_fac"), 1)
                dve.wait_ge(sem("s_fac"), pr + 1)
                v.tensor_scalar(Sx[:, 0:NS], Sx[:, 0:NS], sm[:, 3:4], None, ALU.mult)
                v.tensor_scalar(Sx[:, NS:], Sx[:, NS:], sm[:, 5:6], None, ALU.mult).then_inc(sem("s_p"), 1)
                dve.wait_ge(sem("o_mm"), pr + 2)
                link(v.tensor_tensor(Om.rearrange("p (k d) -> p k d", k=NKV),
                                     ps[:, 5, 0:KVC].rearrange("p (k d) -> p k d", k=NKV),
                                     rowkv.unsqueeze(2).to_broadcast([P, NKV, HD]), ALU.mult))
                for j in range(2):
                    ins = v.tensor_reduce(Od[:, j, :], Om.rearrange("p (k d) -> p d k", k=NKV), AXX, ALU.add)
                ins.then_inc(sem("o_ready"), 1)
                dve.wait_ge(sem("ot_mm"), pr + 1)
                ov = ps[:, 4, 0:P].rearrange("p (b a q g t) -> p a q g b t", b=2, a=2, q=2, g=G)
                for q in range(2):
                    s = slice(64 * q, 64 * q + 64)
                    for a2 in range(2):
                        dst = OT[s, 4 * a2:4 * a2 + 4, bass.ds(pr * 8 + TP, 8)].rearrange("p g (b t) -> p g b t", b=2)
                        ins = v.tensor_copy(dst, ov[s, a2, q])
                ins.then_inc(sem("ot_ev"), 1)
                link.end(PAIRS)
            for j in range(4):
                dve.wait_ge(slot_used, START["wout"] + j + 1)
                ins = v.tensor_tensor(hT[:, 2 * j:2 * j + 2, :], hT[:, 2 * j:2 * j + 2, :], ps[:, 2 * j:2 * j + 2, 0:T],
                                      ALU.add)
            ins.then_inc(sem("wout_done"), 1)
            dve.wait_ge(sem("wout_done"), 1)
            norm(4, sqM)
            dve.wait_ge(sem("in_moe"), 6 * 16)
            dve.wait_ge(sem("rt_mm"), 1)
            tiles = [(t, n) for t, (_, n) in enumerate(TILES)]
            for t, n in tiles:
                ins = v.tensor_copy(lg[0:n, t, :], ps[0:n, 4, 8 * t:8 * t + 8])
            link(ins)
            for t, n in tiles:
                ins = v.tensor_reduce(m8[0:n, t, 0:1], lg[0:n, t, :], AXX, ALU.max, negate=True)
            ins.then_inc(sem("rt_max"), 1)
            for t, n in tiles:
                L = lg[0:n, t, :]
                si, sj = L.unsqueeze(2).to_broadcast([n, 8, 8]), L.unsqueeze(1).to_broadcast([n, 8, 8])
                A = diag[0:n, 0, 0:64].rearrange("p (a b) -> p a b", a=8)
                B = diag[0:n, 1, 0:64].rearrange("p (a b) -> p a b", a=8)
                v.tensor_tensor(A, sj, si, ALU.is_gt)
                link(v.tensor_tensor(B, sj, si, ALU.is_equal))
                link(v.tensor_tensor(B, B, earl8[0:n].rearrange("p (a b) -> p a b", a=8), ALU.mult))
                link(v.tensor_tensor(A, A, B, ALU.add))
                link(v.tensor_reduce(rk8[0:n, t, :], A, AXX, ALU.add))
                link(v.tensor_scalar(mk8[0:n, t, :], rk8[0:n, t, :], 2.0, None, ALU.is_lt))
            v.memset(small[:, 6:7], 0.0).then_inc(sem("mk_ready"), 1)
            dve.wait_ge(sem("rt_exp"), 1)
            for t, n in tiles:
                link(v.tensor_tensor(pe8[0:n, t, :], pe8[0:n, t, :], mk8[0:n, t, :], ALU.mult))
                link(v.tensor_reduce(m8[0:n, t, 1:2], pe8[0:n, t, :], AXX, ALU.add))
                link(v.reciprocal(m8[0:n, t, 1:2], m8[0:n, t, 1:2]))
                link(v.tensor_scalar(comb[0:n, t, :], pe8[0:n, t, :], m8[0:n, t, 1:2], None, ALU.mult))
            dve.wait_ge(sem("pfx_mm"), 1)
            for t, n in tiles:
                link(v.tensor_scalar(pfx[0:n, t, :], ps[0:n, 5, 8 * t:8 * t + 8], 1.0, None, ALU.add))
                link(v.tensor_tensor(pfx[0:n, t, :], pfx[0:n, t, :], mk8[0:n, t, :], ALU.mult))
                link(v.tensor_scalar(pfx[0:n, t, :], pfx[0:n, t, :], -1.0, None, ALU.add))
                for r in range(4):
                    m = 8 if r < 3 else 1
                    v.tensor_tensor(posm[0:n, t, 8 * r:8 * r + m], pfx[0:n, t, 0:m], roff[0:n, 8 * r:8 * r + m],
                                    ALU.subtract)
            v.tensor_reduce(flagf, ps[:, 5, 24:32], AXX, ALU.max).then_inc(sem("cnt_ready"), 1)
            dve.wait_ge(sem("cnt_ready"), 1)
            v.tensor_scalar(flag, flagf, float(P), None, ALU.is_gt).then_inc(sem("flag_ready"), 1)
            i = 0
            for t, (t0, n) in enumerate(TILES):
                for src, dst in [(pfx, posb), (comb, cwb)]:
                    if i:
                        dve.wait_ge(sem("bc_mm"), i)
                    v.tensor_tensor(diag[0:n, :, 0:n], ident[0:n, 0:n].unsqueeze(1).to_broadcast([n, NE, n]),
                                    src[0:n, t, :].unsqueeze(2).to_broadcast([n, NE, n]), ALU.mult)\
                     .then_inc(sem("bc_diag"), 1)
                    dve.wait_ge(sem("bc_mm"), i + 1)
                    ins = v.tensor_copy(dst[:, :, t0:t0 + n].rearrange("p (a b) t -> p a b t", a=2),
                                        ps[:, 6:8, 0:4 * n].rearrange("p a (b t) -> p a b t", b=4))
                    ins.then_inc(sem("bc_ev"), 1)
                    i += 1
            dve.wait_ge(sem("bc_ev"), 6)

            def choose(col):
                for t, n in tiles:
                    ins = v.tensor_scalar(Se[0:n, t, :], iotar[0:n, :],
                                          posm[0:n, t, bass.ds(col, 1)] if not isinstance(col, int)
                                          else posm[0:n, t, col:col + 1], None, ALU.is_equal)
                ins.then_inc(sem("se_ready"), 1)

            choose(0)

            def experts(e, turn, rnd):
                dve.wait_ge(sem("xe_mm"), turn + 1)
                dve.wait_ge(sem("se_ready"), turn + 1)
                choose(turn + 1)
                for u in range(11):
                    g = turn * 11 + u
                    dve.wait_ge(sem("gu_exp"), g + 1)
                    x, bk = ee[:, u % 2], 2 + u % 2
                    link(v.tensor_scalar_add(x, x, 1.0))
                    link(v.reciprocal(x, x))
                    link(v.tensor_tensor(x, x, ps[:, bk, 0:2 * P].rearrange("p (a b) -> p a b", a=2), ALU.mult))
                    if u == 0:
                        dve.wait_ge(slot_used, turn * EPAD + M0)
                    v.tensor_tensor(He[:, 2 * u:2 * u + 2, :], x,
                                    ps[:, bk, 2 * P:].rearrange("p (a b) -> p a b", a=2), ALU.mult)\
                     .then_inc(sem("gu_ev"), 1)
                dve.wait_ge(sem("o_ex"), turn * 4 + 1)
                v.scalar_tensor_tensor(out=SwT.unsqueeze(1), in0=posb[:, bass.ds(e, 1), :], scalar=rnd,
                                       in1=cwb[:, bass.ds(e, 1), :], op0=ALU.is_equal, op1=ALU.mult)\
                 .then_inc(sem("sw_ready"), 1)
                for j in range(4):
                    dve.wait_ge(sem("o_ex"), turn * 4 + (j + 2))
                    v.tensor_tensor(hT[:, 2 * j:2 * j + 2, :], hT[:, 2 * j:2 * j + 2, :],
                                    ps[:, 6:8, 0:T], ALU.add).then_inc(sem("h_ex"), 1)
                dve.wait_ge(sem("h_ex"), turn * 4 + 5)
            with dve.Fori(0, NE, 1) as e:
                link.loop(e, 33)
                experts(e, e, iotac[:, 0:1])
                link.end(NE)
            dve.wait_ge(sem("flag_ready"), 1)
            over = dve.value_load(flag[0:1, 0:1], min_val=0, max_val=1)
            with dve.If(over):
                with dve.Fori(1, 3, 1) as r:
                    with dve.Fori(0, NE, 1) as e:
                        turn = r * NE + e
                        saved = link.n
                        link.n, link.off = saved - NE * 33, turn * 33
                        experts(e, turn, iotac[:, bass.ds(r, 1)])
                        link.n, link.off = saved, None
            fin = Link(dve, "final_chain")
            fin(v.tensor_tensor(sqM, hT, hT, ALU.mult))
            v.memset(small[:, 7:8], 0.0).then_inc(sem("norm_sq"), 1)
            dve.wait_ge(sem("norm_root"), 6)
            fin(v.reciprocal(rstd, rstd))
            for c in range(KD):
                ins = v.scalar_tensor_tensor(out=xnT[:, c, :], in0=hT[:, c, :], scalar=vec[:, FIN + c:FIN + c + 1],
                                             in1=rstd, op0=ALU.mult, op1=ALU.mult)
            ins.then_inc(sem("norm_out"), 1)

        @block.tensor
        def _(pe):
            mm, tr = nc.tensor.matmul, nc.tensor.transpose
            pe.wait_ge(sem("in_ident"), 16)
            pe.wait_ge(sem("in_vec"), 11 * 16)
            tr(ps[:, 0, 0:96], vrow[0:96, 0, :], ident[0:96, 0:96])
            tr(ps[:, 0, 128:252], vrow[0:124, 1, :], ident[0:124, 0:124])
            tr(ps[:, 0, 256:380], vrow[0:124, 2, :], ident[0:124, 0:124]).then_inc(sem("vec_mm"), 1)
            pe.wait_ge(sem("in_x"), 5 * 16)
            for c in range(KD):
                if c >= 2:
                    pe.wait_ge(sem("x_ev"), c - 1)
                for j in range(2):
                    tr(ps[:, 5 + c % 2, 120 * j:120 * j + 120], scn[0:120, j, c * P:(c + 1) * P], ident[0:120, 0:120])
                for t, (t0, n) in enumerate(TILES):
                    ins = tr(ps[:, 1 + c % 4, t0:t0 + n], xnat[0:n, t, c * P:(c + 1) * P], ident[0:n, 0:n])
                ins.then_inc(sem("x_mm"), 1)

            def norm(n, sq, bank=0):
                pe.wait_ge(sem("norm_sq"), n + 1)
                for c in range(KD):
                    ins = mm(ps[:, bank, 0:T], ones, sq[:, c, :], start=(c == 0), stop=(c == KD - 1))
                ins.then_inc(sem("norm_sum"), 1)
                pe.wait_ge(sem("norm_out"), n + 1)

            pe.wait_ge(sem("ones"), 1)
            pe.wait_ge(sem("vec_ready"), 1)
            norm(0, acc)

            def slot(g):
                s, n = need[g]
                pe.wait_ge(full[s], n)
                return ring[:, s, :]

            def cols_view(s):
                return s.rearrange("p (k n) -> p k n", k=KD)

            def linear(w, c, dst, rhs):
                for k in range(KD):
                    ins = mm(dst, w[:, k, c * P:(c + 1) * P], rhs[:, k, :], start=(k == 0), stop=(k == KD - 1))
                return ins

            def gated(name, g0, units, first, second):
                for u in range(units):
                    if u >= 2:
                        pe.wait_ge(sem(name + "_ev"), u - 1)
                    bk = 4 * (u % 2)
                    for j, off in enumerate((first, second)):
                        w = cols_view(slot(g0 + 2 * u + j))
                        for c in range(2):
                            ins = linear(w, c, ps[:, bk + off + c, 0:T], xnT)
                        ins.then_inc(slot_used, 1)

            gated("pw1", START["pw1"], 4, 0, 2)
            pe.wait_ge(sem("pw1_ev"), 4)
            for c in range(KD):
                ins = tr(ps[0:30, c // 4, (c % 4) * P:(c % 4 + 1) * P], fullP[:, c, TP:TP + 30], ident)
            ins.then_inc(sem("convo_mm"), 1)
            pe.wait_ge(sem("tail_ready"), 1)
            for j in range(2):
                for c in range(KD):
                    ins = tr(ps[0:120, 2 + 2 * j + c // 4, (c % 4) * P:(c % 4 + 1) * P],
                             tail[:, c, 120 * j:120 * j + 120], ident)
                ins.then_inc(sem("convo_mm"), 1)
            pe.wait_ge(sem("conv_done"), 1)
            for c in range(KD):
                ins = mm(ps[:, 6, 0:T], ones, acc[:, c, :], start=(c == 0), stop=(c == KD - 1))
            ins.then_inc(sem("ln_sum"), 1)
            pe.wait_ge(sem("ln_centred"), 1)
            for c in range(KD):
                ins = mm(ps[:, 7, 0:T], ones, sqL0[:, c, :], start=(c == 0), stop=(c == KD - 1))
            ins.then_inc(sem("ln_sum"), 1)
            pe.wait_ge(sem("swish_ready"), 1)
            pe.wait_ge(sem("convout_ready"), 3)

            def projection(g0, rhs):
                for j in range(4):
                    w = cols_view(slot(g0 + j))
                    for c in range(2):
                        ins = linear(w, c, ps[:, 2 * j + c, 0:T], rhs)
                    ins.then_inc(slot_used, 1)
            projection(START["pw2"], xnT)
            norm(1, acc)
            gated("ffn", START["ffn"], 11, 0, 2)
            pe.wait_ge(sem("ffn_ev"), 11)
            for k in range(11):
                w = slot(START["down"] + k).rearrange("p (k n) -> p k n", k=2)
                for kk in range(2):
                    for c in range(KD):
                        ins = mm(ps[:, c, 0:T], w[:, kk, c * P:(c + 1) * P], Hf[:, 2 * k + kk, :],
                                 start=(k == 0 and kk == 0), stop=(k == 10 and kk == 1))
                ins.then_inc(slot_used, 1)
            norm(2, acc)
            for j in range(6):
                if j >= 2:
                    pe.wait_ge(sem("kv_ev"), j - 1)
                w = cols_view(slot(START["kv"] + j))
                bk = 4 * (j % 2)
                for t, (t0, n) in enumerate(TILES):
                    for k in range(KD):
                        ins = mm(ps[0:n, bk + t, 0:KVC], xnT[:, k, t0:t0 + n], w[:, k, :],
                                 start=(k == 0), stop=(k == KD - 1))
                ins.then_inc(slot_used, 1)
            pe.wait_ge(sem("kv_ev"), 6)
            for kvi in range(2):
                pe.wait_ge(sem("pos_red"), 2 * kvi + 2)
                mm(ps[:, 3, kvi:kvi + 1], ptmp[:, kvi, 0, :], ones[:, 0:1], start=True, stop=False)
                mm(ps[:, 3, kvi:kvi + 1], ptmp[:, kvi, 1, :], ones[:, 0:1], start=False, stop=True)\
                    .then_inc(sem("pos_mm"), 1)
            pe.wait_ge(sem("pb_ready"), 1)

            def hidden(n, kvi, x, dst, in_sem, in_count):
                pe.wait_ge(in_sem, in_count)
                for d in range(32):
                    ins = mm(dst, w1[:, kvi, d, :], x[:, :, :, d], start=(d == 0), stop=(d == 31))
                ins.then_inc(sem("cmp_used"), 1)

            def project(n, kvi, rows):
                pe.wait_ge(sem("ch_ready"), n + 1)
                for pr in range(2):
                    for q in range(2):
                        k = 2 * pr + q
                        h = chid[:, kvi, k * rows:(k + 1) * rows]
                        if kvi == 0:
                            ins = mm(ps[64 * q:64 * q + 64, 4, pr * rows:(pr + 1) * rows], w2[:, 0, :], h,
                                     start=True, stop=True)
                        else:
                            ins = mm(ps[0:rows, 5, k * HD:(k + 1) * HD], h, w2[:, 1, :], start=True, stop=True)
                ins.then_inc(sem("co_mm"), 1)

            pe.sem_inc(sem("cmp_used"), 2)
            with pe.Fori(0, NB, 1) as b:
                for kvi in range(2):
                    x = cmpbuf[kvi][:, 32:32 + NBLK * KVC].rearrange("p (b k d) -> p k b d", b=NBLK, k=NKV)
                    hidden(b * 2 + kvi, kvi, x, ps[:, kvi, 0:P], sem(f"cmp_in{kvi}"), b * 512 + 512)
                    project(b * 2 + kvi, kvi, NBLK)
                    pe.wait_ge(sem("co_ev"), b * 2 + kvi + 1)
            pe.wait_ge(sem("cp_in"), 32)
            for kvi in range(2):
                x = cpbuf[:, 32:].rearrange("p (b s k d) -> p s k b d", b=4, s=2, k=NKV)[:, kvi]
                hidden(2 * NB + kvi, kvi, x, ps[:, kvi, 0:16], sem("cp_in"), 32)
                project(2 * NB + kvi, kvi, 4)
            pe.wait_ge(sem("co_ev"), 2 * NB + 2)
            for s in range(2):
                for pr in range(2):
                    for t, (t0, n) in enumerate(TILES):
                        c0 = (2 + 2 * s) * KVC + pr * P
                        ins = tr(ps[:, 4 + 2 * s + pr, t0:t0 + n], kv[0:n, t, c0:c0 + P], ident[0:n, 0:n])
                ins.then_inc(sem("kt_mm"), 1)
            norm(3, sq3)
            for j in range(4):
                w = cols_view(slot(START["win"] + j))
                for c in range(2):
                    for k in range(KD):
                        ins = mm(ps[:, 2 * j + c, 0:T], w[:, k, c * P:(c + 1) * P], xnT[:, k, :], start=(k == 0), stop=(k == KD - 1))
                ins.then_inc(slot_used, 1)
            pe.wait_ge(sem("q_ev"), 4)
            pe.wait_ge(sem("kt_ev"), 2)
            pe.wait_ge(sem("in_att"), 20 * 16)
            for t, (t0, n) in enumerate(TILES):
                for k in range(KD):
                    ins = mm(ps[0:n, t, 0:GC], xnT[:, k, t0:t0 + n], wgate[:, k, :], start=(k == 0), stop=(k == KD - 1))
            ins.then_inc(sem("gate_mm"), 1)
            pe.wait_ge(sem("rb_ready"), 1)
            mm(ps[0:NH, 3, 0:TOE], rel33, ohtoe, start=True, stop=True).then_inc(sem("toe_mm"), 1)
            for j in range(8):
                mm(ps[:, 4, j * NH:(j + 1) * NH], ohcp[:, j, :], rel33[0:NBK, :], start=True, stop=True)
            mm(ps[:, 5, 0:1], RB, lastb, start=True, stop=True).then_inc(sem("bias_mm"), 1)
            pe.wait_ge(sem("gate_ready"), 1)
            for pr in range(PAIRS):
                mm(ps[:, 6, pr * GC:(pr + 1) * GC], rowt[:, pr, :], gateP[0:TSN, 2, :], start=True, stop=True)\
                    .then_inc(sem("gs_mm"), 1)

            def unit(u):
                return (u // 4, (u // 2) % 2, u % 2)

            pe.wait_ge(sem("prep_done"), 1)
            pe.wait_ge(sem("toe_in"), 16)
            for j in range(8):
                ins = mm(ps[:, j, :], flip, Tflip[:, 2 * j:2 * j + 2, :].rearrange("p a b -> p (a b)"),
                         start=True, stop=True)
            ins.then_inc(sem("flip_mm"), 1)
            pe.sem_inc(sem("pa_o"), 1)
            with pe.Fori(0, G, 1) as g:
                pe.wait_ge(sem("pa_q"), g + 1)
                pe.wait_ge(sem("pa_o"), g * 8 + 1)

                def qk(u):
                    pr, q, qt = unit(u)
                    nk, w, s = P * (qt + 1), u % 2, slice(64 * q, 64 * q + 64)
                    lhs = qst[s, pr, qt * P:(qt + 1) * P]
                    if u >= 2:
                        pe.wait_ge(sem("pa_max"), g * 8 + (u - 1))
                    for br in range(2):
                        mm(ps[:, w, br * nk:(br + 1) * nk], lhs, KT[s, br, pr, 0:nk], start=True, stop=True)
                    mm(ps[:, 6 + w, 0:4], lhs, kcTp[s, pr, :], start=True, stop=True).then_inc(sem("pa_qk"), 1)

                def trp(u):
                    pr, q, qt = unit(u)
                    w = u % 2
                    pe.wait_ge(sem("pa_p"), g * 8 + (u + 1))
                    if u >= 2:
                        pe.wait_ge(sem("pa_o"), g * 8 + u)
                    i = 0
                    for br in range(2):
                        for kt in range(qt + 1):
                            tr(ps[:, 2 + w, i * P:(i + 1) * P], Sp[:, w, br, kt * P:(kt + 1) * P], ident)
                            i += 1
                    tr(ps[0:4, 4 + w, 0:P], Sc[:, w, :], ident).then_inc(sem("pa_tr"), 1)

                def pv(u):
                    pr, q, qt = unit(u)
                    w, s = u % 2, slice(64 * q, 64 * q + 64)
                    pe.wait_ge(sem("pa_pt"), g * 8 + (u + 1))
                    dst = ps[s, 4 + w, P:2 * P]
                    k = 2 * pr + q
                    i = 0
                    for br in range(2):
                        c0 = (3 + 2 * br) * KVC + k * HD
                        for kt in range(qt + 1):
                            mm(dst, kv[:, kt, c0:c0 + HD], PTp[:, w, i, :], start=(i == 0), stop=False)
                            i += 1
                    mm(dst, vcp[:, k * HD:(k + 1) * HD], PTc[:, w, :], start=False, stop=True).then_inc(sem("pa_pv"), 1)
                qk(0)
                for u in range(8):
                    if u < 7:
                        qk(u + 1)
                    trp(u)
                    pv(u)
            pe.wait_ge(sem("prompt_done"), 1)
            pe.sem_inc(sem("o_mm"), 1)
            pe.sem_inc(sem("s_unit"), 1)
            with pe.Fori(0, PAIRS, 1) as pr:
                pe.wait_ge(sem("st_ready"), pr + 1)
                for b2 in range(2):
                    for a2 in range(2):
                        r0 = 64 * b2 + 32 * a2
                        mm(ps[r0:r0 + 32, 6, 0:NBLK], Qst[:, b2, a2, :], kcs[:, a2, b2, :], start=True, stop=False,
                           skip_group_check=True)
                mm(ps[:, 6, 0:NBLK], RB, ohs[:, WIN + TSN:], start=False, stop=True, skip_group_check=True)\
                    .then_inc(sem("sc_mm"), 1)

                def ktr(u):
                    kt, b2 = u // 2, u % 2
                    slot_ = u % 5
                    pe.wait_ge(sem(f"k_in{slot_}"), pr * 128 + 64 * (u // 5 + 1))
                    pe.wait_ge(sem("kt_out"), pr * 10 + (5 + max(u - 1, 0)))
                    bk = 2 * (u % 2)
                    for a2 in range(2):
                        for n in range(4):
                            ins = tr(ps[:, bk + a2, n * P:(n + 1) * P], Kr[:, slot_, n, a2 * P:(a2 + 1) * P], ident)
                    ins.then_inc(sem("kt_tr"), 1)
                    return ins

                def scores(u):
                    kt, b2 = u // 2, u % 2
                    bk = 4 + kt % 2
                    pe.wait_ge(sem("kt_out"), pr * 10 + (5 + u + 1))
                    if b2 == 0 and kt >= 2:
                        pe.wait_ge(sem("s_ev"), pr * 5 + (kt - 1))
                    biased = kt >= 3
                    for a2 in range(2):
                        r0 = 64 * b2 + 32 * a2
                        ins = mm(ps[r0:r0 + 32, bk, :], Qst[:, b2, a2, :], KTs[:, u % 2, a2, :], start=True,
                                 stop=not biased, skip_group_check=True)
                    if biased and b2 == 1:
                        ins = mm(ps[:, bk, :], RB, ohs[:, 0:WIN], start=False, stop=True, skip_group_check=True)
                    ins.then_inc(sem("s_unit"), 1)

                ktr(0)
                for u in range(10):
                    if u < 9:
                        ktr(u + 1)
                    scores(u)
                    if u == 1:
                        pe.wait_ge(sem("pc_ready"), pr + 1)
                        mm(ps[:, 6, 32:32 + NBLK], samekv, Pcs, start=True, stop=True).then_inc(sem("imp_mm"), 1)
                for j in range(2):
                    for b2 in range(2):
                        for a2 in range(2):
                            r0 = 64 * b2 + 32 * a2
                            mm(ps[r0:r0 + 32, 7, 32 * j:32 * j + 32], Qst[:, b2, a2, :], KT[:, j, a2, TP:T],
                               start=True, stop=False, skip_group_check=True)
                    ins = mm(ps[:, 7, 32 * j:32 * j + 32], RB, ohs[:, WIN:WIN + TSN], start=False, stop=True,
                             skip_group_check=True)
                ins.then_inc(sem("s_new"), 1)
                NS = PAST + TSN
                pe.wait_ge(sem("s_p"), pr + 1)
                offs = [i * P for i in range(16)] + [NS + i * P for i in range(4)]
                for c in range(5):
                    if c == 4:
                        pe.wait_ge(sem("pt_out"), pr * 6 + 1)
                    for i in range(4):
                        o = offs[4 * c + i]
                        ins = tr(ps[:, c % 4, i * P:(i + 1) * P], Sx[:, o:o + P], ident)
                    ins.then_inc(sem("pt_tr"), 1)
                for j, src in enumerate([Sx[:, PAST:PAST + TSN], Sx[:, NS + WIN:NS + WIN + TSN], Scs]):
                    ins = tr(ps[0:TSN, 4, j * P:(j + 1) * P], src, ident)
                ins.then_inc(sem("pt_tr"), 1)
                pe.wait_ge(sem("pt_out"), pr * 6 + 6)
                pe.wait_ge(sem("v_in"), pr * 640 + 640)
                for b2 in range(2):
                    r = slice(64 * b2, 64 * b2 + 64)
                    dst = ps[r, 5, 0:KVC]
                    for i in range(20):
                        mm(dst, PT[:, i, r], V[:, b2, i, :], start=(i == 0), stop=False)
                    for j in range(2):
                        mm(dst, PTn[:, j, r], kv[0:TSN, 2, (3 + 2 * j) * KVC:(4 + 2 * j) * KVC], start=False, stop=False)
                    ins = mm(dst, PTn[:, 2, r], vcs[:, b2, :], start=False, stop=True)
                ins.then_inc(sem("o_mm"), 1)
                pe.wait_ge(sem("o_ready"), pr + 1)
                tr(ps[:, 4, 0:P], Od.rearrange("p a d -> p (a d)"), ident).then_inc(sem("ot_mm"), 1)
                pe.wait_ge(sem("ot_ev"), pr + 1)
            for j in range(4):
                w = slot(START["wout"] + j).rearrange("p (k n) -> p k n", k=KD)
                for c in range(2):
                    ins = linear(w, c, ps[:, 2 * j + c, 0:T], OT)
                ins.then_inc(slot_used, 1 if j < 3 else 1 + M0 - NPRE)
            pe.wait_ge(sem("wout_done"), 1)
            norm(4, sqM)
            pe.wait_ge(sem("in_moe"), 6 * 16)
            for t, (t0, n) in enumerate(TILES):
                for k in range(KD):
                    ins = mm(ps[0:n, 4, 8 * t:8 * t + 8], xnT[:, k, t0:t0 + n], wr[:, k, :], start=(k == 0),
                             stop=(k == KD - 1))
            ins.then_inc(sem("rt_mm"), 1)
            for t, (t0, n) in enumerate(TILES):
                if t == 2:
                    pe.wait_ge(sem("xr_ev"), 1)
                for c in range(KD):
                    ins = tr(ps[0:n, 2 * (t % 2) + c // 4, (c % 4) * P:(c % 4 + 1) * P], xnT[:, c, t0:t0 + n], ident)
                ins.then_inc(sem("xr_mm"), 1)
            pe.wait_ge(sem("mk_ready"), 1)
            for t, (t0, n) in enumerate(TILES):
                for s in range(t + 1):
                    m = TILES[s][1]
                    lhs = before[0:n, 0:n] if s == t else ones[0:m, 0:n]
                    mm(ps[0:n, 5, 8 * t:8 * t + 8], lhs, mk8[0:m, s, :], start=(s == 0), stop=(s == t))
            for s in range(3):
                m = TILES[s][1]
                ins = mm(ps[:, 5, 24:32], ones[0:m, :], mk8[0:m, s, :], start=(s == 0), stop=(s == 2))
            ins.then_inc(sem("pfx_mm"), 1)
            i = 0
            for t, (t0, n) in enumerate(TILES):
                for _ in range(2):
                    pe.wait_ge(sem("bc_diag"), i + 1)
                    if i:
                        pe.wait_ge(sem("bc_ev"), i)
                    for j in range(2):
                        for e in range(4):
                            ins = mm(ps[:, 6 + j, e * n:(e + 1) * n], ones[0:n, :], diag[0:n, 4 * j + e, 0:n],
                                     start=True, stop=True)
                    ins.then_inc(sem("bc_mm"), 1)
                    i += 1
            pe.wait_ge(sem("xr_ev"), 3)
            pe.wait_ge(sem("bc_ev"), 6)

            def gather(n_se):
                pe.wait_ge(sem("se_ready"), n_se)
                for c in range(KD):
                    for t, (t0, n) in enumerate(TILES):
                        ins = mm(ps[:, c // 4, (c % 4) * P:(c % 4 + 1) * P], Xn[0:n, t, c * P:(c + 1) * P], Se[0:n, t, :],
                                 start=(t == 0), stop=(t == 2))
                ins.then_inc(sem("xe_mm"), 1)

            def experts(turn):
                def eslot(k):
                    s = k % RING
                    pe.wait_ge(full[s], turn * (16 * per[s]) + (counts[s] + 16 * (k // RING + 1)))
                    return ring[:, s, :]
                pe.wait_ge(sem("xe_ev"), turn + 1)
                for u in range(11):
                    pe.wait_ge(sem("gu_ev"), turn * 11 + (u + 1))
                    bk = 2 + u % 2
                    for j in range(2):
                        w = cols_view(eslot(2 * u + j))
                        for c in range(2):
                            dst = ps[:, bk, (2 * j + c) * P:(2 * j + c + 1) * P]
                            for k in range(KD):
                                ins = mm(dst, w[:, k, c * P:(c + 1) * P], XeT[:, k, :], start=(k == 0), stop=(k == KD - 1))
                        ins.then_inc(slot_used, 1)
                pe.wait_ge(sem("gu_ev"), turn * 11 + 13)
                for k in range(11):
                    w = eslot(22 + k).rearrange("p (k n) -> p k n", k=2)
                    for kk in range(2):
                        for c in range(2):
                            ins = mm(ps[:, 4 + c, :], He[:, 2 * k + kk, :], w[:, kk, 512 * c:512 * (c + 1)],
                                     start=(k == 0 and kk == 0), stop=(k == 10 and kk == 1))
                    ins.then_inc(slot_used, 1 if k < 10 else 1 + EPAD - 33)
                gather(turn + 2)
                pe.wait_ge(sem("y_ev"), turn + 1)
                pe.wait_ge(sem("sw_ready"), turn + 1)
                for j in range(4):
                    pe.wait_ge(sem("h_ex"), turn * 4 + (j + 1))
                    for c in range(2):
                        cc = 2 * j + c
                        ins = mm(ps[:, 6 + c, 0:T], Ye[:, cc * P:(cc + 1) * P], SwT, start=True, stop=True)
                    ins.then_inc(sem("o_ex"), 1)

            gather(1)
            pe.sem_inc(sem("gu_ev"), 2)
            pe.sem_inc(sem("h_ex"), 1)
            pe.sem_inc(sem("o_ex"), 1)
            with pe.Fori(0, NE, 1) as e:
                experts(e)
            pe.wait_ge(sem("flag_ready"), 1)
            over = pe.value_load(flag[0:1, 0:1], min_val=0, max_val=1)
            with pe.If(over):
                with pe.Fori(1, 3, 1) as r:
                    with pe.Fori(0, NE, 1) as e:
                        experts(r * NE + e)
            norm(5, sqM, 4)
            for t, (t0, n) in enumerate(TILES):
                for c in range(KD):
                    ins = tr(ps[0:n, 2 + 2 * t + c // 4, (c % 4) * P:(c % 4 + 1) * P], xnT[:, c, t0:t0 + n], ident)
                ins.then_inc(sem("yo_mm"), 1)


ARENA = 207 * 1024

_OUTS = [("y_prompt", (1, TP, D)), ("y_sample", (NB, TS, D)), ("kv_prompt", (1, TP, 4, NKV, HD)),
         ("win_prompt", (1, TP, 2, NKV, HD)), ("conv_prompt", (1, 1, CW - 1, D)), ("kv_sample", (NB, TS, 4, NKV, HD)),
         ("win_sample", (NB, WIN, 2, NKV, HD)), ("conv_sample", (1, NB, CW - 1, D))]


def kernel(**inputs):
    import numpy as _np
    import concourse.bacc as _bacc
    from concourse import mybir as _mybir
    from concourse.bass_utils import run_bass_kernel_spmd as _run

    nc = _bacc.Bacc("TRN2", target_bir_lowering=False, num_devices=1)
    arrays, aps = {}, {}
    for name, x in {**inputs, **constants()}.items():
        x = _np.ascontiguousarray(x)
        arrays["in_" + name] = x
        aps[name] = nc.dram_tensor("in_" + name, x.shape, _mybir.dt.from_np(x.dtype), kind="ExternalInput").ap()
    outs = {name: nc.dram_tensor("out_" + name, shape, F32, kind="ExternalOutput").ap() for name, shape in _OUTS}
    build(nc, aps, outs)
    r = _run(nc, [arrays], core_ids=[0])
    return tuple(r.results[0]["out_" + name] for name, _ in _OUTS)
```

```python
import math
from contextlib import ExitStack

import numpy as np

import concourse.bass as bass
from concourse import mybir

F32 = mybir.dt.float32
I32 = mybir.dt.int32
ALU = mybir.AluOpType
ACT = mybir.ActivationFunctionType
AXX = mybir.AxisListType.X

P = 128
D = 1024
KD = D // P
TP, NB, TS = 256, 8, 4
TSN = NB * TS
T = TP + TSN
TILES = [(0, 128), (128, 128), (256, 32)]
PAST, PAGE, NPG, NPHYS = 2048, 128, 16, 160
CW = 31
NH, HD, NKV, G = 16, 64, 4, 4
KVC = NKV * HD
BLOCK, TOPN, WIN = 64, 16, 512
NBLK = PAST // BLOCK
NSB = NBLK + 1
NBK = 32
DFF, FC = 2816, 22
NE = 8
GC = 3 * NH
EPS, NEG, TINY, FORCE = 1e-6, -1e30, 1e-30, 1e4
PAIRS = NB // 2
RING = 5
SLOT = 2048
EPAD = 35
TOE = 2 * P + P - 1


def bucket(dist):
    n = np.maximum(dist, 0)
    nf = np.maximum(n, 1).astype(np.float32)
    large = 16 + (np.log(nf / 16) / math.log(128 / 16) * 16).astype(np.int32)
    return np.where(n < 16, n, np.minimum(large, NBK - 1))


def constants():
    c = {}
    c["ident"] = np.eye(P)
    c["flip"] = np.eye(P)[::-1]
    y = np.arange(TOE)
    oh = np.zeros((NBK + 1, TOE))
    dist = 255 - y
    oh[bucket(dist)[dist >= 0], y[dist >= 0]] = 1
    oh[NBK, dist < 0] = 1
    c["oh_toe"] = oh
    q = np.arange(TP)
    ohc = np.zeros((NBK, 2, 4, P))
    mc = np.zeros((P, 2, 4))
    for qt in range(2):
        for n in range(4):
            d = q[qt * P:(qt + 1) * P] - (n * BLOCK + BLOCK - 1)
            ohc[bucket(d), qt, n, np.arange(P)] = 1
            mc[:, qt, n] = d >= 0
    c["oh_cmp_p"] = ohc.reshape(NBK, -1)
    c["mask_cmp_p"] = mc.reshape(P, -1)
    r = np.arange(P)
    rb, rh, rt = r // 64, (r // 4) % 16, r % 4

    def onehot(pos):
        m = np.zeros((4, NBK, len(pos)))
        for t in range(4):
            m[t, bucket(PAST + t - pos), np.arange(len(pos))] += 1
            m[t, NBK - 1] -= 1
        return m.reshape(P, -1)
    c["oh_smp"] = np.concatenate([onehot(np.arange(PAST - WIN, PAST)),
                                  onehot(PAST + np.arange(TSN) % TS),
                                  onehot(np.arange(NBLK) * BLOCK + BLOCK - 1)], 1)
    c["last_bucket"] = (np.arange(P) % NBK == NBK - 1).astype(float)[:, None]
    c["own_token"] = (np.arange(P)[:, None] // NBK == np.arange(4)[None]).astype(float)
    kb, kt = np.arange(TSN) // TS, np.arange(TSN) % TS
    mn = np.zeros((P, PAIRS, TSN))
    sel = np.zeros((TSN, PAIRS, P))
    for pr in range(PAIRS):
        mn[:, pr] = np.where((kb[None] == 2 * pr + rb[:, None]) & (kt[None] <= rt[:, None]), 0, NEG)
        sel[(2 * pr + rb) * TS + rt, pr, r] = 1
    c["mask_new"] = mn.reshape(P, -1)
    c["row_token"] = sel.reshape(TSN, -1)
    c["mask_win"] = np.where(np.arange(4)[None] >= rt[:, None], 0, NEG)
    c["row_head"] = (rh[:, None] == np.arange(16)[None]).astype(float)
    c["row_kv"] = (rh[:, None] // 4 == np.arange(4)[None]).astype(float)
    c["same_kv"] = ((r[:, None] // 16 == r[None] // 16) & (rt[:, None] == rt[None])).astype(float)
    i = np.arange(NSB)
    c["earlier"] = np.broadcast_to((i[None] < i[:, None]).reshape(1, -1), (P, NSB * NSB))
    c["before"] = (np.arange(P)[:, None] < np.arange(P)[None]).astype(float)
    c["iota_row"] = np.broadcast_to(np.arange(P)[None], (P, P))
    c["earlier8"] = np.broadcast_to((np.arange(8)[None] < np.arange(8)[:, None]).reshape(1, -1), (P, 64))
    c["round_off"] = np.broadcast_to(P * (np.arange(25) // 8)[None], (P, 25))
    c = {k: np.ascontiguousarray(v, np.float32) for k, v in c.items()}
    c["sequences"] = np.arange(NB, dtype=np.int32)[None]
    return c


def build(nc, a, out):
    ctx = ExitStack()
    with ctx:
        sem_names = {}

        def sem(name):
            if name not in sem_names:
                sem_names[name] = ctx.enter_context(nc.semaphore(name))
            return sem_names[name]

        base0 = ctx.enter_context(nc.sbuf_tensor("arena", [P, ARENA // 4], F32))
        cursor = [0]

        def view(off, *shape, parts=P):
            n = int(np.prod(shape))
            assert off * 4 + n * 4 <= ARENA, (off, shape)
            v = base0[0:parts, off:off + n]
            if len(shape) == 1:
                return v
            names = "abcde"[:len(shape)]
            kw = {names[i]: shape[i] for i in range(len(shape))}
            return v.rearrange(f"p ({' '.join(names)}) -> p {' '.join(names)}", **kw)

        def take(*shape, parts=P):
            off = cursor[0]
            cursor[0] += int(np.prod(shape))
            return view(off, *shape, parts=parts)

        ring = take(RING, SLOT)
        hT = take(KD, T)
        XNT = cursor[0]
        xnT = take(KD, T)
        OT = xnT
        vec = take(96 + 248)
        ident = take(P)
        ones = take(P)
        eps = take(1)
        rstd = take(T)
        kv = take(3, 6 * KVC)
        QT = take(KD, T)
        kcT = take(2, NB, NBLK)
        vc = take(NB, KVC, parts=NBLK)
        kcTp = take(2, 2, 4)
        vcp = take(KVC, parts=4)
        small = take(64)
        gsc = take(4)
        pagesI = base0[0:1, cursor[0]:cursor[0] + P].bitcast(I32)
        cursor[0] += P
        seqI = base0[0:1, cursor[0]:cursor[0] + NB].bitcast(I32)
        cursor[0] += NB
        KT = take(2, 2, T)
        R1 = cursor[0]

        def phase():
            cursor[0] = R1

        kvflat = kv.rearrange("p a b -> p (a b)")
        NFP, NFS = KD * (CW - 1 + TP), KD * NB * (CW - 1 + TS)
        fullP = kvflat[:, 0:NFP].rearrange("p (c t) -> p c t", c=KD)
        fullS = kvflat[:, NFP:NFP + NFS].rearrange("p (c b t) -> p c b t", c=KD, b=NB)
        sqc = kvflat[:, 0:KD * T].rearrange("p (c t) -> p c t", c=KD)
        acc = QT
        e0 = KT
        tail = xnT.rearrange("p a b -> p (a b)")[:, 0:KD * 240].rearrange("p (a b) -> p a b", a=KD)
        phase()
        w1 = take(2, 32, P)
        cursor[0] = R1
        xnat = take(3, D)
        scn = take(2, D, parts=120)
        vrow = take(3, P)
        cursor[0] = R1 + 2 * 32 * P
        pos = take(2, 32)
        w2 = take(2, HD)
        pbias = take(2)
        chid = take(2, P)
        CB = cursor[0]
        cmpbuf = [take(NBLK * KVC) for _ in range(2)]
        top_cmp = cursor[0]
        cursor[0] = CB
        Hf = take(FC, T)
        convo = take(3, D)
        top_l0 = cursor[0]
        assert top_l0 <= CB + 16448
        CC = ARENA // 4 - 3400
        cursor[0] = CC
        ohs = take(WIN + TSN + NBLK)
        RB = take(P)
        rel4 = take(NH)
        lastb = take(1)
        ownt = take(4)
        maskn = take(PAIRS, TSN)
        maskw = take(4)
        rowh = take(NH)
        rowkv = take(4)
        samekv = take(P)
        earlier = take(NSB, NSB)
        b31 = take(1)
        gateS = take(PAIRS, 3)
        Qbd = take(NB, 2, 2, G, TS)
        gateP = take(3, GC)
        maskc = take(2, 4)
        biasc = take(2, 4, NH)
        wr = take(KD, NE)
        iotar = take(P)
        before = take(P)
        earl8 = take(64)
        roff = take(25)
        assert cursor[0] * 4 <= ARENA
        C1 = CC - 2900
        cursor[0] = C1
        ohtoe = take(TOE, parts=NBK + 1)
        rel33 = take(NH, parts=NBK + 1)
        ohcp = take(8, P, parts=NBK)
        wgate = take(KD, GC)
        toe = take(TOE, parts=NH)
        flip = take(P)
        rowt = take(PAIRS, P, parts=TSN)
        assert cursor[0] <= CC and C1 >= top_l0
        phase()
        Sx = take(PAST + TSN + WIN + TSN)
        PT = take(20, P)
        PTn = take(3, P, parts=TSN)
        qtflat = QT.rearrange("p a b -> p (a b)")
        KTs = qtflat[:, 0:2048].rearrange("p (a b c) -> p a b c", a=2, b=2)
        Om = qtflat[:, 2048:2048 + KVC]
        Qst = take(2, 2, 32)
        kcs = take(2, 2, NBLK)
        vcs = take(2, KVC, parts=NBLK)
        Scs = take(NBLK)
        Pcs = take(NBLK)
        score = take(NSB)
        rank = take(NSB)
        selb = take(NSB)
        sm = take(8)
        smx = take(7)
        Od = take(2, HD)
        mnst = take(TSN)
        V = take(2, 20, KVC)
        KO = cursor[0]
        Kr = take(5, 4, KVC)
        top_sa = cursor[0]
        assert top_sa <= CC
        cmpA = view(R1, NSB, NSB)
        cmpB = view(R1 + NSB * NSB, NSB, NSB)
        TF = CB + KD * T
        Tflip = view(TF, NH, 2 * P)
        xnQ = view(CB, KD, T)
        cpbuf = view(TF + NH * 2 * P, 32 + 4 * 2 * KVC)
        assert TF + NH * 2 * P + 32 + 4 * 2 * KVC <= C1
        phase()
        Tb = take(NH, 2 * P)
        qst = take(2, TP)
        Sp = take(2, 2, 2, 2 * P)
        Sc = take(2, 2, 4)
        mp = take(2, 6)
        sp = take(2, 6)
        PTp = take(2, 8, P)
        PTc = take(2, 2, P, parts=4)
        top_pa = cursor[0]
        assert top_pa <= KO
        phase()
        Xn = take(3, D)
        XeT = take(KD, P)
        He = take(FC, P)
        Ye = take(D)
        ee = take(2, 2, P)
        Se = take(3, P)
        Sw = take(3, P)
        SwT = take(T)
        lg = take(3, NE)
        pe8 = take(3, NE)
        rk8 = take(3, NE)
        m8 = take(3, 8)
        mk8 = take(3, NE)
        comb = take(3, NE)
        pfx = take(3, NE)
        posm = take(3, 25)
        rkA = take(3, NE, NE)
        rkB = take(3, NE, NE)
        flag = base0[:, cursor[0]:cursor[0] + 1].bitcast(I32)
        flagf = base0[:, cursor[0] + 1:cursor[0] + 2]
        cursor[0] += 2
        sqM = take(KD, T)
        yout = take(3, D)
        top_moe = cursor[0]
        assert top_moe <= CC
        sizes = dict(l0=top_l0, cmp=top_cmp, pa=top_pa, sa=top_sa, moe=top_moe)
        assert max(sizes.values()) * 4 <= ARENA, (sizes, ARENA // 4)

        ps = ctx.enter_context(nc.psum_tensor("ps", [P, 8, 512], F32))
        toe_dram = nc.dram_tensor("toe_scratch", [NH, TOE], F32, kind="Internal").ap()

        MIX0, MIX1, FFN0, FFN1, KVN, FIN, BPW1, BDW, LNG, LNB, BPW2 = 0, 8, 16, 24, 32, 40, 48, 64, 72, 80, 88
        NORM = [MIX0, FFN0, KVN, FFN1, FIN]
        TAP = 96

        plan = []

        def cols(w, c0, slot, n=256):
            return [(slot[:, 0:KD * n].rearrange("p (k n) -> p k n", k=KD),
                     w[:, c0:c0 + n].rearrange("(k p) n -> p k n", p=P))]

        def rows2(w, k):
            return lambda slot: [(slot.rearrange("p (k n) -> p k n", k=2),
                                  w[k * 2 * P:(k + 1) * 2 * P, :].rearrange("(k p) n -> p k n", p=P))]

        for j in range(4):
            for half in range(2):
                plan.append(lambda s, c=half * D + j * 256: cols(a["conv_w_pw1"][0], c, s))
        for j in range(4):
            plan.append(lambda s, c=j * 256: cols(a["conv_w_pw2"][0], c, s))
        for u in range(11):
            for w in ("ffn_w_gate", "ffn_w_up"):
                plan.append(lambda s, w=w, c=u * 256: cols(a[w][0], c, s))
        for k in range(11):
            plan.append(rows2(a["ffn_w_down"][0], k))
        for j in range(6):
            plan.append(lambda s, c=j * 256: cols(a["w_kv"], c, s))

        def win_slot(s, pr, gg):
            w = a["nsa_w_in"][0]
            v = s.rearrange("p (k g q d) -> p k g q d", k=KD, g=2, q=2)
            return [(v[:, :, g2, q, :], w[:, c0:c0 + HD].rearrange("(k p) n -> p k n", p=P))
                    for q in range(2) for g2 in range(2)
                    for c0 in [512 * pr + 256 * q + HD * (2 * gg + g2)]]
        for pr in range(2):
            for gg in range(2):
                plan.append(lambda s, pr=pr, gg=gg: win_slot(s, pr, gg))

        def wout_slot(s, c0):
            w = a["nsa_w_out"][0][:, c0:c0 + 256].rearrange("(p q g d) n -> p q d g n", p=2, q=2, g=4)
            v = s.rearrange("x (p g n) -> x p g n", p=2, g=4)
            return [(v[64 * q:64 * q + 64, pr], w[pr, q]) for pr in range(2) for q in range(2)]
        for j in range(4):
            plan.append(lambda s, c=j * 256: wout_slot(s, c))
        NPRE = len(plan)
        full = [sem(f"ring_full{s}") for s in range(RING)]
        counts, need = [0] * RING, []
        for g, f in enumerate(plan):
            s = g % RING
            counts[s] += 16 * len(f(ring[:, s, :]))
            need.append((s, counts[s]))
        per = [len(range(s, 33, RING)) for s in range(RING)]
        M0 = -(-NPRE // RING) * RING
        START = dict(pw1=0, pw2=8, ffn=12, down=34, kv=45, win=51, wout=55)
        assert START["wout"] + 4 == NPRE

        slot_used = sem("slot_used")

        class Link:

            def __init__(self, eng, name):
                self.eng, self.sem, self.n, self.off = eng, sem(name), 0, None

            def __call__(self, ins):
                self.n += 1
                ins.then_inc(self.sem, 1)
                self.eng.wait_ge(self.sem, self.n if self.off is None else self.off + self.n)
                return ins

            def loop(self, i, per_turn):
                self.start, self.per, self.off = self.n, per_turn, i * per_turn

            def end(self, turns):
                assert self.n - self.start == self.per, (self.n - self.start, self.per)
                self.n, self.off = self.start + self.per * turns, None

        class Dyn:

            def __init__(self, i, per):
                self.i, self.per = i, per

            def __call__(self, n):
                return self.i * self.per + n

        SPLIT = 9

        def cmp_page(eng, name, kvi, n, pg):
            for blk in range(2):
                src = a["cache_kv"][bass.ds(pg, 1), BLOCK * blk:BLOCK * (blk + 1), kvi].rearrange("g l k d -> (g l) (k d)")
                src = bass.AP(tensor=src.tensor, offset=src.offset, ap=[[HD // 2, 2]] + [list(x) for x in src.ap])
                at = (2 * n + blk) * KVC
                eng.dma_start(cmpbuf[kvi][:, at:at + KVC], src).then_inc(sem(f"{name}{kvi}"), 16)

        block = ctx.enter_context(nc.Block())

        @block.sync
        def _(sp):
            def weights(g0, g1):
                for g in range(g0, g1):
                    if g >= RING:
                        sp.wait_ge(slot_used, g - RING + 1)
                    s = g % RING
                    for dst, src in plan[g](ring[:, s, :]):
                        sp.dma_start(dst, src).then_inc(full[s], 16)

            def page(at):
                return sp.value_load(pagesI[0:1, bass.ds(at, 1) if not isinstance(at, int) else slice(at, at + 1)],
                                     min_val=0, max_val=NPHYS - 1)

            for t, (t0, n) in enumerate(TILES):
                src = a["x_prompt"][0, t0:t0 + n] if t < 2 else a["x_sample"].rearrange("b t d -> (b t) d")
                sp.dma_start(xnat[0:n, t, :], src).then_inc(sem("in_x"), 16)
            for j in range(2):
                sp.dma_start(scn[:, j, :], a["state_conv"][0, 4 * j:4 * j + 4].rearrange("b r d -> (b r) d"))\
                   .then_inc(sem("in_x"), 16)
            sp.wait_ge(sem("in_vec"), 11 * 16)
            weights(0, RING)
            sp.dma_start(pagesI, a["page_table"].rearrange("b n -> (b n)").unsqueeze(0)).then_inc(sem("pt_in"), 16)
            sp.dma_start(seqI, a["sequences"]).then_inc(sem("pt_in"), 16)
            sp.wait_ge(sem("pt_in"), 32)
            pages = [page(n) for n in range(SPLIT)]
            for n, pg in enumerate(pages):
                cmp_page(sp, "cmp_in", 0, n, pg)
            weights(RING, 8)
            for n, pg in enumerate(pages):
                cmp_page(sp, "cmp_in", 1, n, pg)
            with sp.Fori(1, NB, 1) as b:
                pages = [page(b * NPG + n) for n in range(SPLIT)]
                for kvi in range(2):
                    sp.wait_ge(sem("cmp_used"), b * 2 + (kvi - 1))
                    for n, pg in enumerate(pages):
                        cmp_page(sp, "cmp_in", kvi, n, pg)
            weights(8, NPRE)

            swin = a["state_win_kv"]

            def keys(pr, u):
                kt, b2, slot = u // 2, u % 2, u % 5
                dst = Kr[:, slot, :, :]
                if kt < 4:
                    for n in range(4):
                        pg = page(pr * 32 + (b2 * NPG + kt * 4 + n))
                        if n == 0:
                            sp.wait_ge(sem("kt_out"), pr * 10 + (u + 1))
                        src = a["cache_kv"][bass.ds(pg, 1), :, 2].rearrange("g l k d -> (g l) (k d)")
                        sp.dma_start(dst[:, n, :], src).then_inc(sem(f"k_in{slot}"), 16)
                else:
                    sq = sp.value_load(seqI[0:1, bass.ds(pr * 2 + b2, 1)], min_val=0, max_val=NB - 1)
                    sp.wait_ge(sem("kt_out"), pr * 10 + (u + 1))
                    w = swin[bass.ds(sq, 1)].rearrange("o (n l) s k d -> l (o n) s (k d)", l=P)
                    sp.dma_start(dst, w[:, :, 0, :]).then_inc(sem(f"k_in{slot}"), 64)

            with sp.Fori(0, PAIRS, 1) as pr:
                for u in range(10):
                    keys(pr, u)

            def experts(e, turn):
                for k in range(33):
                    sp.wait_ge(slot_used, turn * EPAD + (M0 + k - RING + 1))
                    slot = ring[:, k % RING, :]
                    if k < 22:
                        w = a["moe_w_up" if k % 2 else "moe_w_gate"][0]
                        c0 = (k // 2) * 256
                        src = w[bass.ds(e, 1), :, c0:c0 + 256].rearrange("e (k p) n -> p (e k) n", p=P)
                        dst = slot.rearrange("p (k n) -> p k n", k=KD)
                    else:
                        r0 = (k - 22) * 2 * P
                        src = a["moe_w_down"][0][bass.ds(e, 1), r0:r0 + 2 * P, :].rearrange(
                            "e (k p) n -> p (e k) n", p=P)
                        dst = slot.rearrange("p (k n) -> p k n", k=2)
                    sp.dma_start(dst, src).then_inc(full[k % RING], 16)

            with sp.Fori(0, NE, 1) as e:
                experts(e, e)
            sp.wait_ge(sem("flag_ready"), 1)
            over = sp.value_load(flag[0:1, 0:1], min_val=0, max_val=1)
            with sp.If(over):
                with sp.Fori(1, 3, 1) as r:
                    with sp.Fori(0, NE, 1) as e:
                        experts(e, r * NE + e)
            for t, (t0, n) in enumerate(TILES):
                sp.wait_ge(sem("y_ready"), t + 1)
                dst = out["y_prompt"][0, t0:t0 + n] if t < 2 else out["y_sample"].rearrange("b t d -> (b t) d")
                sp.dma_start(dst, yout[0:n, t, :]).then_inc(sem("y_stored"), 16)
            sp.wait_ge(sem("y_stored"), 48)

        @block.gpsimd
        def _(gp):
            nc.gpsimd.memset(gsc, 0.0).then_inc(sem("held"), 1)

            def hold(n):
                gp.wait_ge(sem("held"), n + 1)
                nc.gpsimd.tensor_tensor(gsc[:, 0:1], gsc[:, 1:2], gsc[:, 2:3], ALU.add).then_inc(sem("held"), 1)

            def page(at):
                return gp.value_load(pagesI[0:1, bass.ds(at, 1) if not isinstance(at, int) else slice(at, at + 1)],
                                     min_val=0, max_val=NPHYS - 1)

            gp.wait_ge(sem("pt_in"), 32)
            pages = [page(n) for n in range(SPLIT, NPG)]
            for kvi in range(2):
                for n, pg in enumerate(pages):
                    cmp_page(gp, "cmp_in_gp", kvi, SPLIT + n, pg)
            gp.wait_ge(sem("pw1_ev"), 4)
            nc.gpsimd.tensor_copy(tail.rearrange("p c (b r) -> p c b r", b=NB), fullS[:, :, :, TS:])\
              .then_inc(sem("tail_ready"), 1)
            with gp.Fori(1, NB, 1) as b:
                pages = [page(b * NPG + n) for n in range(SPLIT, NPG)]
                for kvi in range(2):
                    gp.wait_ge(sem("cmp_used"), b * 2 + (kvi - 1))
                    hold(b * 2 + (kvi - 2))
                    for n, pg in enumerate(pages):
                        cmp_page(gp, "cmp_in_gp", kvi, SPLIT + n, pg)
            gp.wait_ge(sem("convout_ready"), 3)
            gp.dma_start(out["conv_prompt"][0, 0], convo[0:30, 0, :]).then_inc(sem("stored"), 16)
            for j in range(2):
                gp.dma_start(out["conv_sample"][0, 4 * j:4 * j + 4].rearrange("b r d -> (b r) d"),
                             convo[0:120, 1 + j, :]).then_inc(sem("stored"), 16)
            gp.wait_ge(sem("stored"), 48)
            swin = a["state_win_kv"]
            gp.wait_ge(sem("prompt_done"), 1)
            gp.wait_ge(sem("pt_in"), 32)
            with gp.Fori(0, PAIRS, 1) as pr:
                gp.wait_ge(sem("o_mm"), pr + 1)
                hold(pr + 2 * (NB - 1))
                for b2 in range(2):
                    for n in range(NPG):
                        pg = page(pr * 32 + (b2 * NPG + n))
                        src = a["cache_kv"][bass.ds(pg, 1), :, 3].rearrange("g l k d -> (g l) (k d)")
                        gp.dma_start(V[:, b2, n, :], src).then_inc(sem("v_in"), 16)
                    w = swin[bass.ds(pr * 2 + b2, 1)].rearrange("o (n l) s k d -> l (o n) s (k d)", l=P)
                    gp.dma_start(V[:, b2, 16:20, :], w[:, :, 1, :]).then_inc(sem("v_in"), 64)

        @block.scalar
        def _(act):
            sc = nc.scalar
            link = Link(act, "act_chain")
            act.dma_start(ident, a["ident"]).then_inc(sem("in_ident"), 16)
            rows = [(a["norm_mix"], 0, 16), (a["norm_ffn"], 16, 16), (a["norm_kv"], 32, 8), (a["norm_final"], 40, 8),
                    (a["conv_b_pw1"], 48, 16), (a["conv_b_dw"], 64, 8), (a["conv_ln_g"], 72, 8),
                    (a["conv_ln_b"], 80, 8), (a["conv_b_pw2"], 88, 8)]
            for v, r0, n in rows:
                src = v.rearrange("(n p) -> n p", p=P) if len(v.shape) == 1 else v.rearrange("a (n p) -> (a n) p", p=P)
                act.dma_start(vrow[r0:r0 + n, 0, :], src).then_inc(sem("in_vec"), 16)
            wdw = a["conv_w_dw"][0].rearrange("w (n p) -> (w n) p", p=P)
            for j in range(2):
                act.dma_start(vrow[0:124, 1 + j, :], wdw[124 * j:124 * j + 124]).then_inc(sem("in_vec"), 16)

            def norm(n, bank=0):
                act.wait_ge(sem("norm_sum"), n + 1)
                sc.activation(rstd, ps[:, bank, 0:T], ACT.Sqrt, scale=1.0 / D, bias=eps).then_inc(sem("norm_root"), 1)

            norm(0)
            act.wait_ge(sem("x_ev"), KD)
            act.wait_ge(sem("vec_mm"), 1)
            for kvi in range(2):
                src = a["cmp_w1"][kvi].rearrange("(l s d) h -> s l d h", s=2, d=32)
                srcp = a["cmp_pos"][kvi].rearrange("l (s d) -> s l d", s=2)
                for s in range(2):
                    act.dma_start(w1[64 * s:64 * s + 64, kvi], src[s]).then_inc(sem("w1_in"), 16)
                    act.dma_start(pos[64 * s:64 * s + 64, kvi], srcp[s]).then_inc(sem("w1_in"), 16)
                act.dma_start(w2[:, kvi, :], a["cmp_w2"][kvi]).then_inc(sem("w1_in"), 16)
            for u in range(4):
                act.wait_ge(slot_used, START["pw1"] + 2 * u + 2)
                if u >= 2:
                    act.wait_ge(sem("pw1_ev"), u - 1)
                bk = 4 * (u % 2)
                for c in range(2):
                    ins = sc.activation(e0[:, u % 2, c, :], ps[:, bk + 2 + c, 0:T], ACT.Sigmoid,
                                        bias=vec[:, BPW1 + 8 + 2 * u + c:BPW1 + 9 + 2 * u + c])
                ins.then_inc(sem("pw1_exp"), 1)
            act.wait_ge(sem("pos_mm"), 1)
            sc.activation(pbias, ps[:, 3, 0:2], ACT.Copy).then_inc(sem("pb_ready"), 1)
            act.wait_ge(sem("pb_ready"), 1)

            def compress(n, kvi, ncol, evacuate):
                act.wait_ge(sem("cmp_used"), n + 1)
                sc.activation(chid[:, kvi, 0:ncol], ps[:, kvi, 0:ncol], ACT.Silu, bias=pbias[:, kvi:kvi + 1])\
                  .then_inc(sem("ch_ready"), 1)
                act.wait_ge(sem("co_mm"), n + 1)
                evacuate().then_inc(sem("co_ev"), 1)

            with act.Fori(0, NB, 1) as b:
                compress(b * 2, 0, P, lambda: sc.activation(
                    kcT[:, :, bass.ds(b, 1), :], ps[:, 4, 0:2 * NBLK].rearrange("p (a o b) -> p a o b", a=2, o=1), ACT.Copy))
                compress(b * 2 + 1, 1, P, lambda: sc.activation(
                    vc[:, bass.ds(b, 1), :], ps[0:NBLK, 5, 0:KVC].unsqueeze(1), ACT.Copy))
            for j in range(3):
                act.wait_ge(sem("convo_mm"), j + 1)
                n = 30 if j == 0 else 120
                sc.activation(convo[0:n, j, :], ps[0:n, 2 * j:2 * j + 2, :].rearrange("p a b -> p (a b)"), ACT.Copy)\
                  .then_inc(sem("convout_ready"), 1)
            act.wait_ge(sem("ln_sum"), 1)
            sc.activation(rstd, ps[:, 6, 0:T], ACT.Copy, scale=1.0 / D).then_inc(sem("ln_mean"), 1)
            act.wait_ge(sem("ln_sum"), 2)
            act.wait_ge(sem("ln_centred"), 2)
            sc.activation(rstd, ps[:, 7, 0:T], ACT.Sqrt, scale=1.0 / D, bias=eps).then_inc(sem("ln_root"), 1)
            for c in range(KD):
                if c % (KD // 2) == 0:
                    act.wait_ge(sem("ln_hat"), 1 + c // (KD // 2))
                sc.activation(xnT[:, c, :], acc[:, c, :], ACT.Silu, scale=vec[:, LNG + c:LNG + c + 1],
                              bias=vec[:, LNB + c:LNB + c + 1]).then_inc(sem("swish_ready"), 1)
            act.wait_ge(sem("cmp_used"), 2 * NB)
            for dst, name in [(ohs, "oh_smp"), (lastb, "last_bucket"), (ownt, "own_token"), (maskw, "mask_win"),
                              (rowh, "row_head"), (rowkv, "row_kv"), (samekv, "same_kv"), (flip, "flip"),
                              (ohtoe, "oh_toe"), (rel33[0:NBK, :], "rel_bias"), (iotar, "iota_row"),
                              (before, "before"), (earl8, "earlier8"), (roff, "round_off")]:
                act.dma_start(dst, a[name]).then_inc(sem("in_att"), 16)
            for dst, name in [(maskn, "mask_new"), (rowt, "row_token"), (earlier, "earlier"), (ohcp, "oh_cmp_p"),
                              (maskc, "mask_cmp_p")]:
                act.dma_start(dst, a[name].rearrange("p (a b) -> p a b", a=dst.shape[1])).then_inc(sem("in_att"), 16)
            for t in range(4):
                act.dma_start(rel4[32 * t:32 * t + 32, :], a["rel_bias"]).then_inc(sem("in_att"), 16)
            act.dma_start(wgate, a["nsa_w_in"][0][:, D:D + GC].rearrange("(k p) n -> p k n", p=P))\
               .then_inc(sem("in_att"), 16)
            act.dma_start(wr, a["moe_w_router"][0].rearrange("(k p) n -> p k n", p=P)).then_inc(sem("in_att"), 16)
            norm(1)
            for u in range(11):
                act.wait_ge(slot_used, START["ffn"] + 2 * u + 2)
                if u >= 2:
                    act.wait_ge(sem("ffn_ev"), u - 1)
                bk = 4 * (u % 2)
                sc.activation(e0[:, u % 2], ps[:, bk:bk + 2, 0:T], ACT.Silu).then_inc(sem("ffn_exp"), 1)
            norm(2)
            act.wait_ge(sem("toe_mm"), 1)
            sc.activation(toe, ps[0:NH, 3, 0:TOE], ACT.Copy).then_inc(sem("toe_ev"), 1)
            act.wait_ge(sem("toe_ev"), 1)
            act.dma_start(toe_dram, toe).then_inc(sem("toe_out"), 16)
            act.wait_ge(sem("toe_out"), 16)
            skew = bass.AP(tensor=toe_dram.tensor, offset=0, ap=[[1, P], [TOE, NH], [1, 2 * P]])
            act.wait_ge(sem("stored"), 48)
            act.dma_start(Tflip, skew).then_inc(sem("toe_in"), 16)
            for j in range(6):
                act.wait_ge(slot_used, START["kv"] + j + 1)
                bk = 4 * (j % 2)
                sc.activation(kv[:, 0:2, j * KVC:(j + 1) * KVC], ps[:, bk:bk + 2, 0:KVC], ACT.Copy)
                sc.activation(kv[0:TSN, 2, j * KVC:(j + 1) * KVC], ps[0:TSN, bk + 2, 0:KVC], ACT.Copy)\
                  .then_inc(sem("kv_ev"), 1)
            act.wait_ge(sem("kv_ev"), 6)
            for t in range(2):
                act.dma_start(out["kv_prompt"][0, t * P:(t + 1) * P].rearrange("t s k d -> t (s k d)"),
                              kv[:, t, 0:4 * KVC]).then_inc(sem("kvp_stored"), 16)
                act.dma_start(out["win_prompt"][0, t * P:(t + 1) * P].rearrange("t s k d -> t (s k d)"),
                              kv[:, t, 4 * KVC:]).then_inc(sem("stored_a"), 16)
            act.dma_start(out["kv_sample"].rearrange("b t s k d -> (b t) (s k d)"), kv[0:TSN, 2, 0:4 * KVC])\
               .then_inc(sem("stored_a"), 16)
            act.dma_start(out["win_sample"][:, WIN - TS:].rearrange("b t s k d -> b t (s k d)"),
                          kv[0:TSN, 2, 4 * KVC:]).then_inc(sem("stored_a"), 16)
            for s in range(2):
                act.wait_ge(sem("kt_mm"), s + 1)
                sc.activation(KT[:, s], ps[:, 4 + 2 * s:6 + 2 * s, 0:T], ACT.Copy).then_inc(sem("kt_ev"), 1)
            act.wait_ge(sem("kvp_stored"), 32)
            srcp = out["kv_prompt"][0][:, 0:2].rearrange("(b l) s k d -> l b (s k d)", b=4)
            for s in range(2):
                off = 32 * (1 - s)
                act.dma_start(cpbuf[64 * s:64 * s + 64, off:off + 4 * 2 * KVC].rearrange("p (b n) -> p b n", b=4),
                              srcp).then_inc(sem("cp_in"), 16)
            for j in range(4):
                act.wait_ge(slot_used, START["win"] + j + 1)
                bk = 2 * (j % 4)
                sc.activation(QT[:, 2 * j:2 * j + 2, :], ps[:, bk:bk + 2, 0:T], ACT.Copy, scale=HD ** -0.5)\
                  .then_inc(sem("q_ev"), 1)
            act.wait_ge(sem("gate_mm"), 1)
            sc.activation(gateP[:, 0:2, :], ps[:, 0:2, 0:GC], ACT.Sigmoid)
            sc.activation(gateP[0:TSN, 2, :], ps[0:TSN, 2, 0:GC], ACT.Sigmoid).then_inc(sem("gate_ready"), 1)
            def keys_out():
                for q in range(2):
                    s = slice(64 * q, 64 * q + 64)
                    ins = sc.activation(kcTp[s, :, q, :], ps[s, 4, 0:8].rearrange("p (a b) -> p a b", a=2), ACT.Copy)
                return ins
            act.wait_ge(sem("kct_zero"), 1)
            compress(2 * NB, 0, 16, keys_out)
            compress(2 * NB + 1, 1, 16, lambda: sc.activation(vcp, ps[0:4, 5, 0:KVC], ACT.Copy))

            def pa_exp(g, u):
                w, nk = u % 2, P * (u % 2 + 1)
                act.wait_ge(sem("pa_max"), g * 4 + (u + 1))
                for q in range(2):
                    for br in range(2):
                        i = 2 * q + br
                        sc.activation(Sp[:, w, q, br, 0:nk], Sp[:, w, q, br, 0:nk], ACT.Exp,
                                      bias=mp[:, w, i:i + 1], accum_out=sp[:, w, i:i + 1])
                for q in range(2):
                    ins = sc.activation(Sc[:, w, q, :], Sc[:, w, q, :], ACT.Exp, bias=mp[:, w, 4 + q:5 + q])
                ins.then_inc(sem("pa_exp"), 1)

            def pa_turn(g, last):
                for u in range(4):
                    if not (last and u == 3):
                        pa_exp(g, u + 1)
                    w, nk = u % 2, P * (u % 2 + 1)
                    act.wait_ge(sem("pa_tr"), g * 4 + (u + 1))
                    sc.activation(PTc[:, w], ps[0:4, 7, P:3 * P].rearrange("p (a b) -> p a b", a=2), ACT.Copy)
                    sc.activation(PTp[:, w].rearrange("p (q i) c -> p q (i c)", q=2)[:, :, 0:2 * nk],
                                  ps[:, 4:6, 0:2 * nk], ACT.Copy).then_inc(sem("pa_pt"), 1)

            act.wait_ge(sem("flip_mm"), 1)
            act.sem_inc(sem("kt_out"), 5)
            act.dma_start(out["win_sample"][:, 0:WIN - TS].rearrange("b w s k d -> b (w s k d)"),
                          a["state_win_kv"][:, TS:WIN].rearrange("b w s k d -> b (w s k d)")).then_inc(sem("stored_a"), 16)
            pa_exp(0, 0)
            with act.Fori(0, G - 1, 1) as g:
                pa_turn(g, False)
            pa_turn(G - 1, True)

            act.wait_ge(sem("prompt_done"), 1)
            with act.Fori(0, PAIRS, 1) as pr:
                act.wait_ge(sem("sc_max"), pr + 1)
                sc.activation(Scs, Scs, ACT.Exp, bias=sm[:, 0:1], accum_out=sm[:, 1:2]).then_inc(sem("sc_exp"), 1)
                for u in range(10):
                    act.wait_ge(sem("kt_tr"), pr * 10 + (u + 1))
                    act.wait_ge(sem("s_unit"), pr * 10 + max(u, 1))
                    bk = 2 * (u % 2)
                    sc.activation(KTs[:, u % 2], ps[:, bk:bk + 2, :], ACT.Copy).then_inc(sem("kt_out"), 1)
                act.wait_ge(sem("s_max"), pr + 1)
                sc.activation(Sx[:, 0:PAST + TSN], Sx[:, 0:PAST + TSN], ACT.Exp, bias=sm[:, 2:3], accum_out=sm[:, 3:4])
                sc.activation(Sx[:, PAST + TSN:], Sx[:, PAST + TSN:], ACT.Exp, bias=sm[:, 4:5], accum_out=sm[:, 5:6])\
                  .then_inc(sem("s_exp"), 1)
                for c in range(5):
                    act.wait_ge(sem("pt_tr"), pr * 6 + (c + 1))
                    sc.activation(PT[:, 4 * c:4 * c + 4, :], ps[:, c % 4, :].rearrange("p (a b) -> p a b", a=4), ACT.Copy)\
                      .then_inc(sem("pt_out"), 1)
                act.wait_ge(sem("pt_tr"), pr * 6 + 6)
                sc.activation(PTn, ps[0:TSN, 4, 0:3 * P].rearrange("p (a b) -> p a b", a=3), ACT.Copy)\
                  .then_inc(sem("pt_out"), 1)
            act.wait_ge(sem("wout_done"), 1)
            norm(3)
            for t, (t0, n) in enumerate(TILES):
                act.wait_ge(sem("xr_mm"), t + 1)
                bk = 2 * (t % 2)
                sc.activation(Xn[0:n, t, :], ps[0:n, bk:bk + 2, :].rearrange("p a b -> p (a b)"), ACT.Copy)\
                  .then_inc(sem("xr_ev"), 1)
            act.wait_ge(sem("rt_max"), 1)
            for t, (t0, n) in enumerate(TILES):
                ins = sc.activation(pe8[0:n, t, :], lg[0:n, t, :], ACT.Exp, bias=m8[0:n, t, 0:1])
            ins.then_inc(sem("rt_exp"), 1)

            act.wait_ge(sem("xe_mm"), 1)
            sc.activation(XeT, ps[:, 0:2, :].rearrange("p a (b c) -> p (a b) c", c=P), ACT.Copy).then_inc(sem("xe_ev"), 1)

            def experts(turn):
                for u in range(11):
                    v = turn * 11 + u
                    act.wait_ge(slot_used, turn * EPAD + (M0 + 2 * u + 2))
                    act.wait_ge(sem("gu_ev"), v + 1)
                    sc.activation(ee[:, u % 2], ps[:, 2 + u % 2, 0:2 * P], ACT.Silu).then_inc(sem("gu_exp"), 1)
                act.wait_ge(sem("sw_tr"), turn + 1)
                sc.activation(SwT, ps[:, 7, 0:T], ACT.Copy).then_inc(sem("sw_ready"), 1)
                act.wait_ge(slot_used, turn * EPAD + (M0 + 33))
                sc.activation(Ye, ps[:, 4:6, :].rearrange("p a b -> p (a b)"), ACT.Copy).then_inc(sem("y_ev"), 1)
                act.wait_ge(sem("xe_mm"), turn + 2)
                sc.activation(XeT, ps[:, 0:2, :].rearrange("p a (b c) -> p (a b) c", c=P), ACT.Copy)\
                  .then_inc(sem("xe_ev"), 1)

            with act.Fori(0, NE, 1) as e:
                experts(e)
            act.wait_ge(sem("flag_ready"), 1)
            over = act.value_load(flag[0:1, 0:1], min_val=0, max_val=1)
            with act.If(over):
                with act.Fori(1, 3, 1) as r:
                    with act.Fori(0, NE, 1) as e:
                        experts(r * NE + e)
            norm(4, 4)
            for t, (t0, n) in enumerate(TILES):
                act.wait_ge(sem("yo_mm"), t + 1)
                bk = 2 + 2 * t
                sc.activation(yout[0:n, t, :], ps[0:n, bk:bk + 2, :].rearrange("p a b -> p (a b)"), ACT.Copy)\
                  .then_inc(sem("y_ready"), 1)
            act.wait_ge(sem("stored_a"), 5 * 16)
            act.wait_ge(sem("kvp_stored"), 2 * 16)

        @block.vector
        def _(dve):
            v = nc.vector
            link = Link(dve, "dve_chain")
            link(v.memset(eps, EPS))
            v.memset(ones, 1.0).then_inc(sem("ones"), 1)
            v.memset(fullP[:, :, 0:CW - 1], 0.0)
            v.memset(kcTp, 0.0).then_inc(sem("kct_zero"), 1)
            for c in range(KD):
                dve.wait_ge(sem("x_mm"), c + 1)
                v.tensor_copy(fullS[:, c, :, 0:CW - 1].rearrange("p (a b) r -> p a b r", a=2),
                              ps[:, 5 + c % 2, 0:240].rearrange("p (a b r) -> p a b r", a=2, b=4))
                link(v.tensor_copy(hT[:, c, :], ps[:, 1 + c % 4, 0:T]))
                v.tensor_tensor(acc[:, c, :], hT[:, c, :], hT[:, c, :], ALU.mult)\
                 .then_inc(sem("x_ev"), 1)
            dve.wait_ge(sem("vec_mm"), 1)
            v.tensor_copy(vec[:, 0:96], ps[:, 7, 0:96])
            v.tensor_copy(vec[:, 96:96 + 124], ps[:, 7, 128:252])
            link(v.tensor_copy(vec[:, 96 + 124:], ps[:, 7, 256:380]))

            def norm_tail(n):
                dve.wait_ge(sem("norm_root"), n + 1)
                link(v.reciprocal(rstd, rstd))
                for c in range(KD):
                    col = NORM[n] + c
                    v.scalar_tensor_tensor(out=xnT[:, c, :], in0=hT[:, c, :], scalar=vec[:, col:col + 1],
                                           in1=rstd, op0=ALU.mult, op1=ALU.mult).then_inc(sem("norm_out"), 1)

            def norm(n, sq):
                for c in (slice(0, KD // 2), slice(KD // 2, KD)):
                    v.tensor_tensor(sq[:, c, :], hT[:, c, :], hT[:, c, :], ALU.mult).then_inc(sem("norm_sq"), 1)
                norm_tail(n)

            norm_tail(0)
            for u in range(4):
                dve.wait_ge(sem("pw1_exp"), u + 1)
                e = e0[:, u % 2]
                for c in range(2):
                    cc = 2 * u + c
                    bk = 4 * (u % 2) + c
                    b = vec[:, BPW1 + cc:BPW1 + cc + 1]
                    v.scalar_tensor_tensor(out=fullP[:, cc, CW - 1:], in0=ps[:, bk, 0:TP], scalar=b,
                                           in1=e[:, c, 0:TP], op0=ALU.add, op1=ALU.mult)
                    ins = v.scalar_tensor_tensor(out=fullS[:, cc, :, CW - 1:],
                                                 in0=ps[:, bk, TP:T].rearrange("p (b t) -> p b t", b=NB), scalar=b,
                                                 in1=e[:, c, TP:T].rearrange("p (b t) -> p b t", b=NB),
                                                 op0=ALU.add, op1=ALU.mult)
                ins.then_inc(sem("pw1_ev"), 1)
            dve.wait_ge(sem("pw1_ev"), 4)
            taps = Link(dve, "tap_chain")
            fP, fS = fullP, fullS
            with dve.Fori(0, KD, 1) as c:
                base = c * (2 * CW)
                aP = acc[:, bass.ds(c, 1), 0:TP]
                aS = acc[:, bass.ds(c, 1), TP:T].rearrange("p o (b t) -> p (o b) t", b=NB)
                for w in range(CW):
                    tap = vec[:, bass.ds(c + (TAP + 8 * w), 1)]
                    for k, (o, f) in enumerate([(aP, fP[:, bass.ds(c, 1), w:w + TP]),
                                                (aS, fS[:, bass.ds(c, 1), :, w:w + TS].rearrange("p o b t -> p (o b) t"))]):
                        if w == 0:
                            ins = v.tensor_scalar(o, f, tap, vec[:, bass.ds(c + BDW, 1)], ALU.mult, ALU.add)
                        else:
                            dve.wait_ge(taps.sem, base + 2 * (w - 1) + k + 1)
                            ins = v.scalar_tensor_tensor(out=o, in0=f, scalar=tap, in1=o, op0=ALU.mult, op1=ALU.add)
                        ins.then_inc(taps.sem, 1)
            dve.wait_ge(taps.sem, KD * 2 * CW)
            v.memset(small[:, 1:2], 0.0).then_inc(sem("conv_done"), 1)
            dve.wait_ge(sem("convo_mm"), 3)
            dve.wait_ge(sem("ln_mean"), 1)
            halves = (slice(0, KD // 2), slice(KD // 2, KD))
            every = rstd.unsqueeze(1).to_broadcast([P, KD // 2, T])
            for c in halves:
                link(v.tensor_tensor(acc[:, c, :], acc[:, c, :], every, ALU.subtract))
                v.tensor_tensor(sqc[:, c, :], acc[:, c, :], acc[:, c, :], ALU.mult).then_inc(sem("ln_centred"), 1)
            dve.wait_ge(sem("ln_root"), 1)
            link(v.reciprocal(rstd, rstd))
            for c in halves:
                v.tensor_tensor(acc[:, c, :], acc[:, c, :], every, ALU.mult).then_inc(sem("ln_hat"), 1)
            for j in range(4):
                dve.wait_ge(slot_used, START["pw2"] + j + 1)
                for c in range(2):
                    cc = 2 * j + c
                    ins = v.scalar_tensor_tensor(out=hT[:, cc, :], in0=ps[:, 2 * j + c, 0:T],
                                                 scalar=vec[:, BPW2 + cc:BPW2 + cc + 1], in1=hT[:, cc, :],
                                                 op0=ALU.add, op1=ALU.add)
                link(ins)
            norm(1, acc)
            for u in range(11):
                dve.wait_ge(sem("ffn_exp"), u + 1)
                e, bk = e0[:, u % 2], 4 * (u % 2)
                v.tensor_tensor(Hf[:, 2 * u:2 * u + 2, :], e, ps[:, bk + 2:bk + 4, 0:T], ALU.mult)\
                 .then_inc(sem("ffn_ev"), 1)
            dve.wait_ge(slot_used, START["down"] + 11)
            link(v.tensor_tensor(hT, hT, ps[:, :, 0:T], ALU.add))
            dve.wait_ge(sem("in_att"), 25 * 16)
            v.memset(rel33[NBK:NBK + 1, :], NEG)
            v.tensor_tensor(RB.rearrange("p (b h t) -> p b h t", b=2, h=NH),
                            rel4.unsqueeze(1).unsqueeze(3).to_broadcast([P, 2, NH, 4]),
                            ownt.unsqueeze(1).unsqueeze(1).to_broadcast([P, 2, NH, 4]), ALU.mult)\
             .then_inc(sem("rb_ready"), 1)
            norm(2, acc)
            for c in range(KD):
                ins = v.scalar_tensor_tensor(out=xnQ[:, c, :], in0=hT[:, c, :], scalar=vec[:, MIX1 + c:MIX1 + c + 1],
                                             in1=rstd, op0=ALU.mult, op1=ALU.mult)
            ins.then_inc(sem("xq_ready"), 1)
            dve.wait_ge(sem("bias_mm"), 1)
            v.tensor_copy(b31, ps[:, 5, 0:1])
            mneg = small[:, 8:16].rearrange("p (a b) -> p a b", a=2)
            link(v.tensor_scalar(mneg, maskc, -1.0, -NEG, ALU.add, ALU.mult))
            link(v.tensor_tensor(biasc, ps[:, 4, 0:8 * NH].rearrange("p (a b c) -> p a b c", a=2, b=4),
                                 mneg.unsqueeze(3).to_broadcast([P, 2, 4, NH]), ALU.add))
            v.memset(Qbd, 0.0).then_inc(sem("prep1"), 1)
            dve.wait_ge(sem("prep1"), 1)
            dve.wait_ge(sem("q_ev"), 4)
            qv = QT[:, :, TP:T].rearrange("p (a g) (b t) -> p a g b t", a=2, b=NB)
            for q in range(2):
                for pr in range(2):
                    s = slice(64 * q, 64 * q + 64)
                    for b in range(2):
                        v.tensor_copy(Qbd[s, 4 * b:4 * b + 4, pr, q],
                                      qv[s, pr, :, 4 * b:4 * b + 4].rearrange("p g b t -> p b g t"))
            for pr in range(PAIRS):
                dve.wait_ge(sem("gs_mm"), PAIRS)
                tmp = small[:, 16:64].rearrange("p (h b) -> p h b", h=NH)
                link(v.tensor_tensor(tmp, ps[:, 6, pr * GC:(pr + 1) * GC].rearrange("p (h b) -> p h b", h=NH),
                                     rowh.unsqueeze(2).to_broadcast([P, NH, 3]), ALU.mult))
                link(v.tensor_reduce(gateS[:, pr, :], tmp.rearrange("p h b -> p b h"), AXX, ALU.add))
            v.memset(small[:, 0:1], 0.0).then_inc(sem("prep_done"), 1)
            dve.wait_ge(sem("flip_mm"), 1)
            v.tensor_copy(Tb.rearrange("p (a b) c -> p a (b c)", a=8), ps[:, :, :]).then_inc(sem("o_mm"), 1)
            dve.wait_ge(sem("o_mm"), 1)

            def unit(u):
                return (u // 2, u % 2)

            def of_pair(x, pr, g):
                g1 = slice(g, g + 1) if isinstance(g, int) else bass.ds(g, 1)
                return x.rearrange("p (a q g) n -> p a q g n", a=2, q=2)[:, pr, :, g1, :]

            gates = [gateP[:, t, :].rearrange("p (h n) -> p h n", h=NH) for t in range(2)]

            def queries(g):
                for pr in range(2):
                    at = g + 4 * pr
                    ins = v.tensor_copy(qst[:, pr:pr + 1, :],
                                        QT[:, slice(at, at + 1) if isinstance(at, int) else bass.ds(at, 1), 0:TP])
                ins.then_inc(sem("pa_q"), 1)

            def front(g, u):
                pr, qt = unit(u)
                nk, w = P * (qt + 1), u % 2
                dve.wait_ge(sem("pa_qk"), g * 4 + (u + 1))
                v.tensor_tensor(Sp[:, w, :, :, 0:nk],
                                ps[:, 2 * w:2 * w + 2, 0:2 * nk].rearrange("p q (b n) -> p q b n", b=2),
                                of_pair(Tb[:, :, 2 * P - nk:], pr, g).to_broadcast([P, 2, 2, nk]), ALU.add)
                bc = of_pair(biasc[:, qt].rearrange("p n h -> p h n"), pr, g)
                link(v.tensor_tensor(Sc[:, w].unsqueeze(2), ps[:, 6, 0:8].rearrange("p (q o n) -> p q o n", q=2, o=1),
                                     bc, ALU.add))
                v.tensor_reduce(mp[:, w, 0:4], Sp[:, w, :, :, 0:nk], AXX, ALU.max, negate=True)
                v.tensor_reduce(mp[:, w, 4:6], Sc[:, w], AXX, ALU.max, negate=True).then_inc(sem("pa_max"), 1)

            def back(g, u):
                pr, qt = unit(u)
                nk, w = P * (qt + 1), u % 2
                dve.wait_ge(sem("pa_exp"), g * 4 + (u + 1))
                link(v.tensor_tensor(Sc[:, w], Sc[:, w], maskc[:, qt, :].unsqueeze(1).to_broadcast([P, 2, 4]), ALU.mult))
                link(v.tensor_reduce(sp[:, w, 4:6], Sc[:, w], AXX, ALU.add))
                link(v.tensor_scalar(sp[:, w, :], sp[:, w, :], TINY, None, ALU.max))
                link(v.reciprocal(sp[:, w, :], sp[:, w, :]))
                gq = of_pair(gates[qt], pr, g)
                v.tensor_tensor(mp[:, w, 0:4].rearrange("p (q o b) -> p q o b", q=2, o=1),
                                sp[:, w, 0:4].rearrange("p (q o b) -> p q o b", q=2, o=1), gq[:, :, :, 1:3], ALU.mult)
                v.tensor_tensor(mp[:, w, 4:6].rearrange("p (q o b) -> p q o b", q=2, o=1),
                                sp[:, w, 4:6].rearrange("p (q o b) -> p q o b", q=2, o=1), gq[:, :, :, 0:1], ALU.mult)\
                 .then_inc(sem("pa_fac"), 1)
                dve.wait_ge(sem("pa_fac"), g * 4 + (u + 1))
                v.tensor_tensor(Sp[:, w, :, :, 0:nk], Sp[:, w, :, :, 0:nk],
                                mp[:, w, 0:4].rearrange("p (q b) -> p q b", q=2).unsqueeze(3).to_broadcast([P, 2, 2, nk]),
                                ALU.mult)
                v.tensor_tensor(Sc[:, w], Sc[:, w], mp[:, w, 4:6].unsqueeze(2).to_broadcast([P, 2, 4]), ALU.mult)\
                 .then_inc(sem("pa_p"), 1)

            def done(g, u):
                pr, qt = unit(u)
                at = g + 4 * pr
                dve.wait_ge(sem("pa_pv"), g * 4 + (u + 1))
                v.tensor_copy(OT[:, slice(at, at + 1) if isinstance(at, int) else bass.ds(at, 1), qt * P:qt * P + P],
                              ps[:, 7, 0:P].unsqueeze(1)).then_inc(sem("pa_o"), 1)

            def pa_turn(g, first, last):
                for u in range(4):
                    if not (last and u == 3):
                        if not (first and u == 0):
                            dve.wait_ge(sem("pa_tr"), g * 4 + u)
                        if u < 3:
                            front(g, u + 1)
                        else:
                            front(g + 1, 0)
                    if u == 2 and not last:
                        queries(g + 1)
                    back(g, u)
                    if u > 0:
                        done(g, u - 1)
                    elif not first:
                        done(g - 1, 3)

            queries(0)
            front(0, 0)
            pa_turn(0, True, False)
            with dve.Fori(1, G - 1, 1) as g:
                link.loop(g - 1, 4 * 5)
                pa_turn(g, False, False)
                link.end(G - 2)
            pa_turn(G - 1, False, True)
            done(G - 1, 3)
            dve.wait_ge(sem("pa_o"), 4 * G + 1)
            v.memset(small[:, 5:6], 0.0).then_inc(sem("prompt_done"), 1)
            link(v.memset(score, FORCE))

            NS = PAST + TSN
            with dve.Fori(0, PAIRS, 1) as pr:
                link.loop(pr, 15)
                v.tensor_copy(Qst, Qbd.rearrange("p b a q g t -> p (b a) (q g t)")[:, bass.ds(pr * 4, 4), :]
                              .rearrange("p (b a) n -> p b a n", b=2))
                v.tensor_copy(kcs, kcT[:, :, bass.ds(pr * 2, 2), :])
                v.tensor_copy(mnst.unsqueeze(1), maskn[:, bass.ds(pr, 1), :])
                v.tensor_copy(vcs, vc[:, bass.ds(pr * 2, 2), :]).then_inc(sem("st_ready"), 1)
                dve.wait_ge(sem("sc_mm"), pr + 1)
                link(v.tensor_scalar(Scs, ps[:, 6, 0:NBLK], b31, None, ALU.add))
                v.tensor_reduce(sm[:, 0:1], Scs, AXX, ALU.max, negate=True).then_inc(sem("sc_max"), 1)
                dve.wait_ge(sem("sc_exp"), pr + 1)
                link(v.tensor_scalar(sm[:, 1:2], sm[:, 1:2], TINY, None, ALU.max))
                link(v.reciprocal(sm[:, 1:2], sm[:, 1:2]))
                v.tensor_scalar(Pcs, Scs, sm[:, 1:2], None, ALU.mult).then_inc(sem("pc_ready"), 1)
                dve.wait_ge(sem("pc_ready"), pr + 1)
                v.tensor_scalar(Scs, Pcs, gateS[:, bass.ds(pr, 1), 0:1].rearrange("p a b -> p (a b)"), None, ALU.mult)
                dve.wait_ge(sem("imp_mm"), pr + 1)
                link(v.tensor_copy(score[:, 1:NBLK - 1], ps[:, 6, 32 + 1:32 + NBLK - 1]))
                si = score.unsqueeze(2).to_broadcast([P, NSB, NSB])
                sj = score.unsqueeze(1).to_broadcast([P, NSB, NSB])
                v.tensor_tensor(cmpA, sj, si, ALU.is_gt)
                link(v.tensor_tensor(cmpB, sj, si, ALU.is_equal))
                link(v.tensor_tensor(cmpB, cmpB, earlier, ALU.mult))
                link(v.tensor_tensor(cmpA, cmpA, cmpB, ALU.add))
                link(v.tensor_reduce(rank, cmpA, AXX, ALU.add))
                link(v.tensor_scalar(selb, rank, float(TOPN), NEG, ALU.is_ge, ALU.mult))
                for kt in range(4):
                    dve.wait_ge(sem("s_unit"), pr * 10 + (2 * kt + 3))
                    bk = 4 + kt % 2
                    v.scalar_tensor_tensor(out=Sx[:, kt * 512:(kt + 1) * 512].rearrange("p (b l) -> p b l", b=8),
                                           in0=ps[:, bk, :].rearrange("p (b l) -> p b l", b=8), scalar=b31,
                                           in1=selb[:, 8 * kt:8 * kt + 8].unsqueeze(2).to_broadcast([P, 8, BLOCK]),
                                           op0=ALU.add, op1=ALU.add).then_inc(sem("s_ev"), 1)
                    dve.wait_ge(sem("s_ev"), pr * 5 + (kt + 1))
                    v.tensor_reduce(smx[:, kt:kt + 1], Sx[:, kt * 512:(kt + 1) * 512], AXX, ALU.max)
                dve.wait_ge(sem("s_unit"), pr * 10 + 11)
                link(v.tensor_scalar(Sx[:, NS:NS + WIN], ps[:, 4, :], b31, None, ALU.add))
                v.tensor_tensor(Sx[:, NS:NS + 4], Sx[:, NS:NS + 4], maskw, ALU.add).then_inc(sem("s_ev"), 1)
                dve.wait_ge(sem("s_ev"), pr * 5 + 5)
                v.tensor_reduce(smx[:, 5:6], Sx[:, NS:NS + WIN], AXX, ALU.max)
                dve.wait_ge(sem("s_new"), pr + 1)
                for j, o in enumerate([PAST, NS + WIN]):
                    ins = v.scalar_tensor_tensor(out=Sx[:, o:o + TSN], in0=ps[:, 7, 32 * j:32 * j + 32], scalar=b31,
                                                 in1=mnst, op0=ALU.add, op1=ALU.add)
                link(ins)
                v.tensor_reduce(smx[:, 4:5], Sx[:, PAST:NS], AXX, ALU.max)
                link(v.tensor_reduce(smx[:, 6:7], Sx[:, NS + WIN:], AXX, ALU.max))
                v.tensor_reduce(sm[:, 2:3], smx[:, 0:5], AXX, ALU.max, negate=True)
                v.tensor_reduce(sm[:, 4:5], smx[:, 5:7], AXX, ALU.max, negate=True).then_inc(sem("s_max"), 1)
                dve.wait_ge(sem("s_exp"), pr + 1)
                for j in range(2):
                    s = sm[:, 3 + 2 * j:4 + 2 * j]
                    ins = v.tensor_scalar(s, s, TINY, None, ALU.max)
                link(ins)
                for j in range(2):
                    s = sm[:, 3 + 2 * j:4 + 2 * j]
                    ins = v.reciprocal(s, s)
                link(ins)
                for j in range(2):
                    s = sm[:, 3 + 2 * j:4 + 2 * j]
                    ins = v.tensor_tensor(s, s, gateS[:, bass.ds(pr, 1), 1 + j:2 + j].rearrange("p a b -> p (a b)"),
                                          ALU.mult)
                ins.then_inc(sem("s_fac"), 1)
                dve.wait_ge(sem("s_fac"), pr + 1)
                for lo, hi, f in [(0, 512, 3), (512, 1024, 3), (1024, 1536, 3), (1536, NS, 3), (NS, NS + WIN + TSN, 5)]:
                    v.tensor_scalar(Sx[:, lo:hi], Sx[:, lo:hi], sm[:, f:f + 1], None, ALU.mult).then_inc(sem("s_p"), 1)
                dve.wait_ge(sem("o_mm"), pr + 2)
                link(v.tensor_tensor(Om.rearrange("p (k d) -> p k d", k=NKV),
                                     ps[:, 5, 0:KVC].rearrange("p (k d) -> p k d", k=NKV),
                                     rowkv.unsqueeze(2).to_broadcast([P, NKV, HD]), ALU.mult))
                for j in range(2):
                    ins = v.tensor_reduce(Od[:, j, :], Om.rearrange("p (k d) -> p d k", k=NKV), AXX, ALU.add)
                ins.then_inc(sem("o_ready"), 1)
                dve.wait_ge(sem("ot_mm"), pr + 1)
                ov = ps[:, 4, 0:P].rearrange("p (b a q g t) -> p a q g b t", b=2, a=2, q=2, g=G)
                for q in range(2):
                    s = slice(64 * q, 64 * q + 64)
                    for a2 in range(2):
                        dst = OT[s, 4 * a2:4 * a2 + 4, bass.ds(pr * 8 + TP, 8)].rearrange("p g (b t) -> p g b t", b=2)
                        ins = v.tensor_copy(dst, ov[s, a2, q])
                ins.then_inc(sem("ot_ev"), 1)
                link.end(PAIRS)
            for j in range(4):
                dve.wait_ge(slot_used, START["wout"] + j + 1)
                ins = v.tensor_tensor(hT[:, 2 * j:2 * j + 2, :], hT[:, 2 * j:2 * j + 2, :], ps[:, 2 * j:2 * j + 2, 0:T],
                                      ALU.add)
            ins.then_inc(sem("wout_done"), 1)
            dve.wait_ge(sem("wout_done"), 1)
            norm(3, sqM)
            link(v.memset(lg, 0.0))
            dve.wait_ge(sem("rt_mm"), 1)
            tiles = [(t, n) for t, (_, n) in enumerate(TILES)]
            v.tensor_copy(lg[:, 0:2, :], ps[:, 4, 0:16].rearrange("p (t e) -> p t e", t=2))
            link(v.tensor_copy(lg[0:TSN, 2, :], ps[0:TSN, 4, 16:24]))
            v.tensor_reduce(m8[:, :, 0:1], lg, AXX, ALU.max, negate=True).then_inc(sem("rt_max"), 1)
            si, sj = lg.unsqueeze(3).to_broadcast([P, 3, NE, NE]), lg.unsqueeze(2).to_broadcast([P, 3, NE, NE])
            link(v.tensor_tensor(rkB, sj, si, ALU.is_equal))
            for t in range(3):
                ins = v.tensor_tensor(rkB[:, t], rkB[:, t], earl8.rearrange("p (a b) -> p a b", a=NE), ALU.mult)
            v.tensor_tensor(rkA, sj, si, ALU.is_gt)
            link(v.memset(small[:, 6:7], 0.0))
            link(v.tensor_tensor(rkA, rkA, rkB, ALU.add))
            link(v.tensor_reduce(rk8, rkA, AXX, ALU.add))
            v.tensor_scalar(mk8, rk8, 2.0, None, ALU.is_lt).then_inc(sem("mk_ready"), 1)
            dve.wait_ge(sem("mk_ready"), 1)
            dve.wait_ge(sem("rt_exp"), 1)
            link(v.tensor_tensor(pe8, pe8, mk8, ALU.mult))
            link(v.tensor_reduce(m8[:, :, 1:2], pe8, AXX, ALU.add))
            link(v.reciprocal(m8[:, :, 1:2], m8[:, :, 1:2]))
            link(v.tensor_tensor(comb, pe8, m8[:, :, 1:2].to_broadcast([P, 3, NE]), ALU.mult))
            dve.wait_ge(sem("pfx_mm"), 1)
            for t, n in tiles:
                link(v.tensor_scalar(pfx[0:n, t, :], ps[0:n, 5, 8 * t:8 * t + 8], 1.0, None, ALU.add))
                link(v.tensor_tensor(pfx[0:n, t, :], pfx[0:n, t, :], mk8[0:n, t, :], ALU.mult))
                link(v.tensor_scalar(pfx[0:n, t, :], pfx[0:n, t, :], -1.0, None, ALU.add))
                for r in range(4):
                    m = 8 if r < 3 else 1
                    v.tensor_tensor(posm[0:n, t, 8 * r:8 * r + m], pfx[0:n, t, 0:m], roff[0:n, 8 * r:8 * r + m],
                                    ALU.subtract)
            v.tensor_reduce(flagf, ps[:, 5, 24:32], AXX, ALU.max).then_inc(sem("cnt_ready"), 1)
            dve.wait_ge(sem("cnt_ready"), 1)
            v.tensor_scalar(flag, flagf, float(P), None, ALU.is_gt).then_inc(sem("flag_ready"), 1)
            def choose(col, e):
                c1 = slice(col, col + 1) if isinstance(col, int) else bass.ds(col, 1)
                for t, n in tiles:
                    ins = v.tensor_scalar(Se[0:n, t, :], iotar[0:n, :], posm[0:n, t, c1], None, ALU.is_equal)
                ins.then_inc(sem("se_ready"), 1)

            def weigh(turn, e):
                for t, n in tiles:
                    ins = v.tensor_scalar(Sw[0:n, t, :], iotar[0:n, :], posm[0:n, t, bass.ds(turn, 1)],
                                          comb[0:n, t, bass.ds(e, 1)], ALU.is_equal, ALU.mult)
                ins.then_inc(sem("sw_made"), 1)

            choose(0, 0)

            def experts(e, turn):
                dve.wait_ge(sem("xe_mm"), turn + 1)
                dve.wait_ge(sem("se_ready"), turn + 1)
                choose(turn + 1, None)
                dve.wait_ge(sem("o_ex"), turn * 4 + 1)
                weigh(turn, e)
                for u in range(11):
                    g = turn * 11 + u
                    dve.wait_ge(sem("gu_exp"), g + 1)
                    x, bk = ee[:, u % 2], 2 + u % 2
                    if u == 0:
                        dve.wait_ge(slot_used, turn * EPAD + M0)
                    v.tensor_tensor(He[:, 2 * u:2 * u + 2, :], x,
                                    ps[:, bk, 2 * P:].rearrange("p (a b) -> p a b", a=2), ALU.mult)\
                     .then_inc(sem("gu_ev"), 1)
                for j in range(4):
                    dve.wait_ge(sem("o_ex"), turn * 4 + (j + 2))
                    v.tensor_tensor(hT[:, 2 * j:2 * j + 2, :], hT[:, 2 * j:2 * j + 2, :],
                                    ps[:, 6 - 2 * (j % 2):8 - 2 * (j % 2), 0:T], ALU.add).then_inc(sem("h_ex"), 1)
                dve.wait_ge(sem("h_ex"), turn * 4 + 4)
            with dve.Fori(0, NE, 1) as e:
                experts(e, e)
            dve.wait_ge(sem("flag_ready"), 1)
            over = dve.value_load(flag[0:1, 0:1], min_val=0, max_val=1)
            with dve.If(over):
                with dve.Fori(1, 3, 1) as r:
                    with dve.Fori(0, NE, 1) as e:
                        turn = r * NE + e
                        experts(e, turn)
            fin = Link(dve, "final_chain")
            for c in halves:
                fin(v.tensor_tensor(sqM[:, c, :], hT[:, c, :], hT[:, c, :], ALU.mult))
                v.memset(small[:, 7:8], 0.0).then_inc(sem("norm_sq"), 1)
            dve.wait_ge(sem("norm_root"), 5)
            fin(v.reciprocal(rstd, rstd))
            for c in range(KD):
                v.scalar_tensor_tensor(out=xnT[:, c, :], in0=hT[:, c, :], scalar=vec[:, FIN + c:FIN + c + 1],
                                       in1=rstd, op0=ALU.mult, op1=ALU.mult).then_inc(sem("norm_out"), 1)

        @block.tensor
        def _(pe):
            mm, tr = nc.tensor.matmul, nc.tensor.transpose
            pe.wait_ge(sem("in_ident"), 16)
            pe.wait_ge(sem("in_x"), 5 * 16)
            for c in range(KD):
                if c >= 2:
                    pe.wait_ge(sem("x_ev"), c - 1)
                for j in range(2):
                    tr(ps[:, 5 + c % 2, 120 * j:120 * j + 120], scn[0:120, j, c * P:(c + 1) * P], ident[0:120, 0:120])
                for t, (t0, n) in enumerate(TILES):
                    ins = tr(ps[:, 1 + c % 4, t0:t0 + n], xnat[0:n, t, c * P:(c + 1) * P], ident[0:n, 0:n])
                ins.then_inc(sem("x_mm"), 1)

            pe.wait_ge(sem("in_vec"), 11 * 16)
            tr(ps[:, 7, 0:96], vrow[0:96, 0, :], ident[0:96, 0:96])
            tr(ps[:, 7, 128:252], vrow[0:124, 1, :], ident[0:124, 0:124])
            tr(ps[:, 7, 256:380], vrow[0:124, 2, :], ident[0:124, 0:124]).then_inc(sem("vec_mm"), 1)

            def norm_sums(n, sq, bank=0):
                for c in range(KD):
                    if n == 0:
                        pe.wait_ge(sem("x_ev"), c + 1)
                    elif c % (KD // 2) == 0:
                        pe.wait_ge(sem("norm_sq"), 2 * (n - 1) + 1 + c // (KD // 2))
                    ins = mm(ps[:, bank, 0:T], ones, sq[:, c, :], start=(c == 0), stop=(c == KD - 1))
                ins.then_inc(sem("norm_sum"), 1)

            fresh = []

            def operand(k):
                if fresh:
                    pe.wait_ge(sem(fresh[0][0]), fresh[0][1] + k + 1)
                    if k == KD - 1:
                        fresh.clear()

            def norm(n, sq, bank=0):
                norm_sums(n, sq, bank)
                fresh.append(("norm_out", KD * n))

            pe.wait_ge(sem("ones"), 1)
            norm(0, acc)

            def slot(g):
                s, n = need[g]
                pe.wait_ge(full[s], n)
                return ring[:, s, :]

            def cols_view(s):
                return s.rearrange("p (k n) -> p k n", k=KD)

            def linear(w, c, dst, rhs):
                for k in range(KD):
                    operand(k)
                    ins = mm(dst, w[:, k, c * P:(c + 1) * P], rhs[:, k, :], start=(k == 0), stop=(k == KD - 1))
                return ins

            def gated(name, g0, units, first, second):
                for u in range(units):
                    if u >= 2:
                        pe.wait_ge(sem(name + "_ev"), u - 1)
                    bk = 4 * (u % 2)
                    for j, off in enumerate((first, second)):
                        w = cols_view(slot(g0 + 2 * u + j))
                        for c in range(2):
                            ins = linear(w, c, ps[:, bk + off + c, 0:T], xnT)
                        ins.then_inc(slot_used, 1)

            gated("pw1", START["pw1"], 4, 0, 2)
            pe.wait_ge(sem("pw1_ev"), 4)
            pe.wait_ge(sem("w1_in"), 10 * 16)
            def hidden(kvi, x, dst):
                for d in range(32):
                    ins = mm(dst, w1[:, kvi, d, :], x[:, :, :, d], start=(d == 0), stop=(d == 31))
                ins.then_inc(sem("cmp_used"), 1)

            def project(n, kvi, rows):
                pe.wait_ge(sem("ch_ready"), n + 1)
                for pr in range(2):
                    for q in range(2):
                        k = 2 * pr + q
                        h = chid[:, kvi, k * rows:(k + 1) * rows]
                        if kvi == 0:
                            ins = mm(ps[64 * q:64 * q + 64, 4, pr * rows:(pr + 1) * rows], w2[:, 0, :], h,
                                     start=True, stop=True)
                        else:
                            ins = mm(ps[0:rows, 5, k * HD:(k + 1) * HD], h, w2[:, 1, :], start=True, stop=True)
                ins.then_inc(sem("co_mm"), 1)

            def cmp_hidden(b):
                for kvi in range(2):
                    x = cmpbuf[kvi].rearrange("p (b k d) -> p k b d", b=NBLK, k=NKV)
                    pe.wait_ge(sem(f"cmp_in{kvi}"), b * (32 * SPLIT) + 32 * SPLIT)
                    pe.wait_ge(sem(f"cmp_in_gp{kvi}"), b * (32 * (NPG - SPLIT)) + 32 * (NPG - SPLIT))
                    hidden(kvi, x, ps[:, kvi, 0:P])

            def cmp_project(b):
                for kvi in range(2):
                    project(b * 2 + kvi, kvi, NBLK)
                pe.wait_ge(sem("co_ev"), b * 2 + 2)

            cmp_hidden(0)
            for kvi in range(2):
                for d in range(32):
                    ins = mm(ps[:, 3, kvi:kvi + 1], w1[:, kvi, d, :], pos[:, kvi, d:d + 1], start=(d == 0),
                             stop=(d == 31))
            ins.then_inc(sem("pos_mm"), 1)

            cmp_project(0)
            with pe.Fori(1, NB, 1) as b:
                cmp_hidden(b)
                cmp_project(b)
            for c in range(KD):
                ins = tr(ps[0:30, c // 4, (c % 4) * P:(c % 4 + 1) * P], fullP[:, c, TP:TP + 30], ident)
            ins.then_inc(sem("convo_mm"), 1)
            pe.wait_ge(sem("tail_ready"), 1)
            for j in range(2):
                for c in range(KD):
                    ins = tr(ps[0:120, 2 + 2 * j + c // 4, (c % 4) * P:(c % 4 + 1) * P],
                             tail[:, c, 120 * j:120 * j + 120], ident)
                ins.then_inc(sem("convo_mm"), 1)
            pe.wait_ge(sem("conv_done"), 1)
            for c in range(KD):
                ins = mm(ps[:, 6, 0:T], ones, acc[:, c, :], start=(c == 0), stop=(c == KD - 1))
            ins.then_inc(sem("ln_sum"), 1)
            for c in range(KD):
                if c % (KD // 2) == 0:
                    pe.wait_ge(sem("ln_centred"), 1 + c // (KD // 2))
                ins = mm(ps[:, 7, 0:T], ones, sqc[:, c, :], start=(c == 0), stop=(c == KD - 1))
            ins.then_inc(sem("ln_sum"), 1)
            pe.wait_ge(sem("convout_ready"), 3)
            fresh.append(("swish_ready", 0))

            def projection(g0, rhs):
                for j in range(4):
                    w = cols_view(slot(g0 + j))
                    for c in range(2):
                        ins = linear(w, c, ps[:, 2 * j + c, 0:T], rhs)
                    ins.then_inc(slot_used, 1)
            projection(START["pw2"], xnT)
            norm(1, acc)
            gated("ffn", START["ffn"], 11, 0, 2)
            pe.wait_ge(sem("ffn_ev"), 11)
            for k in range(11):
                w = slot(START["down"] + k).rearrange("p (k n) -> p k n", k=2)
                for kk in range(2):
                    for c in range(KD):
                        ins = mm(ps[:, c, 0:T], w[:, kk, c * P:(c + 1) * P], Hf[:, 2 * k + kk, :],
                                 start=(k == 0 and kk == 0), stop=(k == 10 and kk == 1))
                ins.then_inc(slot_used, 1)
            norm_sums(2, acc)
            pe.wait_ge(sem("in_att"), 25 * 16)
            pe.wait_ge(sem("rb_ready"), 1)
            mm(ps[0:NH, 3, 0:TOE], rel33, ohtoe, start=True, stop=True).then_inc(sem("toe_mm"), 1)
            for j in range(8):
                mm(ps[:, 4, j * NH:(j + 1) * NH], ohcp[:, j, :], rel33[0:NBK, :], start=True, stop=True)
            mm(ps[:, 5, 0:1], RB, lastb, start=True, stop=True).then_inc(sem("bias_mm"), 1)
            fresh.append(("norm_out", 2 * KD))
            for j in range(6):
                if j == 1:
                    pe.wait_ge(sem("prep1"), 1)
                if j >= 2:
                    pe.wait_ge(sem("kv_ev"), j - 1)
                w = cols_view(slot(START["kv"] + j))
                bk = 4 * (j % 2)
                for t, (t0, n) in enumerate(TILES):
                    for k in range(KD):
                        operand(k)
                        ins = mm(ps[0:n, bk + t, 0:KVC], xnT[:, k, t0:t0 + n], w[:, k, :],
                                 start=(k == 0), stop=(k == KD - 1))
                ins.then_inc(slot_used, 1)
            pe.wait_ge(sem("kv_ev"), 6)
            for s in range(2):
                for pr in range(2):
                    for t, (t0, n) in enumerate(TILES):
                        c0 = (2 + 2 * s) * KVC + pr * P
                        ins = tr(ps[:, 4 + 2 * s + pr, t0:t0 + n], kv[0:n, t, c0:c0 + P], ident[0:n, 0:n])
                ins.then_inc(sem("kt_mm"), 1)
            pe.wait_ge(sem("xq_ready"), 1)
            for j in range(4):
                if j == 2:
                    pe.wait_ge(sem("kt_ev"), 2)
                w = cols_view(slot(START["win"] + j))
                for c in range(2):
                    for k in range(KD):
                        ins = mm(ps[:, 2 * j + c, 0:T], w[:, k, c * P:(c + 1) * P], xnQ[:, k, :], start=(k == 0), stop=(k == KD - 1))
                ins.then_inc(slot_used, 1)
            pe.wait_ge(sem("q_ev"), 2)
            for t, (t0, n) in enumerate(TILES):
                for k in range(KD):
                    ins = mm(ps[0:n, t, 0:GC], xnQ[:, k, t0:t0 + n], wgate[:, k, :], start=(k == 0), stop=(k == KD - 1))
            ins.then_inc(sem("gate_mm"), 1)
            pe.wait_ge(sem("gate_ready"), 1)
            for pr in range(PAIRS):
                mm(ps[:, 6, pr * GC:(pr + 1) * GC], rowt[:, pr, :], gateP[0:TSN, 2, :], start=True, stop=True)\
                    .then_inc(sem("gs_mm"), 1)

            pe.wait_ge(sem("cp_in"), 32)
            for kvi in range(2):
                x = cpbuf[:, 32:].rearrange("p (b s k d) -> p s k b d", b=4, s=2, k=NKV)[:, kvi]
                hidden(kvi, x, ps[:, kvi, 0:16])
            for kvi in range(2):
                project(2 * NB + kvi, kvi, 4)
            pe.wait_ge(sem("co_ev"), 2 * NB + 2)

            def unit(u):
                return (u // 2, u % 2)

            pe.wait_ge(sem("prep_done"), 1)
            pe.wait_ge(sem("toe_in"), 16)
            for j in range(8):
                ins = mm(ps[:, j, :], flip, Tflip[:, 2 * j:2 * j + 2, :].rearrange("p a b -> p (a b)"),
                         start=True, stop=True)
            ins.then_inc(sem("flip_mm"), 1)
            pe.sem_inc(sem("pa_o"), 1)

            def qk(g, u):
                pr, qt = unit(u)
                nk, w = P * (qt + 1), u % 2
                for br in range(2):
                    for q in range(2):
                        s = slice(64 * q, 64 * q + 64)
                        mm(ps[:, 2 * w + q, br * nk:(br + 1) * nk], qst[s, pr, qt * P:(qt + 1) * P],
                           KT[s, br, pr, 0:nk], start=True, stop=True)
                mm(ps[:, 6, 0:8], qst[:, pr, qt * P:(qt + 1) * P], kcTp[:, pr].rearrange("p a b -> p (a b)"),
                   start=True, stop=True).then_inc(sem("pa_qk"), 1)

            def trp(g, u):
                pr, qt = unit(u)
                w = u % 2
                pe.wait_ge(sem("pa_p"), g * 4 + (u + 1))
                for q in range(2):
                    i = 0
                    for br in range(2):
                        for kt in range(qt + 1):
                            tr(ps[:, 4 + q, i * P:(i + 1) * P], Sp[:, w, q, br, kt * P:(kt + 1) * P], ident)
                            i += 1
                pe.wait_ge(sem("pa_o"), g * 4 + (u + 1))
                for q in range(2):
                    ins = tr(ps[0:4, 7, P + P * q:2 * P + P * q], Sc[:, w, q, :], ident)
                ins.then_inc(sem("pa_tr"), 1)

            def pv(g, u):
                pr, qt = unit(u)
                w = u % 2
                pe.wait_ge(sem("pa_pt"), g * 4 + (u + 1))
                i = 0
                for br in range(2):
                    for kt in range(qt + 1):
                        for q in range(2):
                            c0 = (3 + 2 * br) * KVC + (2 * pr + q) * HD
                            mm(ps[64 * q:64 * q + 64, 7, 0:P], kv[:, kt, c0:c0 + HD], PTp[:, w, 4 * q + i, :],
                               start=(i == 0), stop=False)
                        i += 1
                for q in range(2):
                    k = 2 * pr + q
                    ins = mm(ps[64 * q:64 * q + 64, 7, 0:P], vcp[:, k * HD:(k + 1) * HD], PTc[:, w, q, :],
                             start=False, stop=True)
                ins.then_inc(sem("pa_pv"), 1)

            def pa_turn(g, last):
                for u in range(4):
                    if not (last and u >= 2):
                        pe.wait_ge(sem("pa_max"), g * 4 + (u + 2))
                        if u < 2:
                            qk(g, u + 2)
                        else:
                            if u == 2:
                                pe.wait_ge(sem("pa_q"), g + 2)
                            qk(g + 1, u - 2)
                    trp(g, u)
                    pv(g, u)

            pe.wait_ge(sem("pa_q"), 1)
            qk(0, 0)
            pe.wait_ge(sem("pa_max"), 1)
            qk(0, 1)
            with pe.Fori(0, G - 1, 1) as g:
                pa_turn(g, False)
            pa_turn(G - 1, True)
            pe.wait_ge(sem("prompt_done"), 1)
            pe.sem_inc(sem("s_unit"), 1)
            with pe.Fori(0, PAIRS, 1) as pr:
                pe.wait_ge(sem("st_ready"), pr + 1)
                for b2 in range(2):
                    for a2 in range(2):
                        r0 = 64 * b2 + 32 * a2
                        mm(ps[r0:r0 + 32, 6, 0:NBLK], Qst[:, b2, a2, :], kcs[:, a2, b2, :], start=True, stop=False,
                           skip_group_check=True)
                mm(ps[:, 6, 0:NBLK], RB, ohs[:, WIN + TSN:], start=False, stop=True, skip_group_check=True)\
                    .then_inc(sem("sc_mm"), 1)

                def ktr(u):
                    kt, b2 = u // 2, u % 2
                    slot_ = u % 5
                    pe.wait_ge(sem(f"k_in{slot_}"), pr * 128 + 64 * (u // 5 + 1))
                    pe.wait_ge(sem("kt_out"), pr * 10 + (5 + max(u - 1, 0)))
                    bk = 2 * (u % 2)
                    for a2 in range(2):
                        for n in range(4):
                            ins = tr(ps[:, bk + a2, n * P:(n + 1) * P], Kr[:, slot_, n, a2 * P:(a2 + 1) * P], ident)
                    ins.then_inc(sem("kt_tr"), 1)
                    return ins

                def scores(u):
                    kt, b2 = u // 2, u % 2
                    bk = 4 + kt % 2
                    pe.wait_ge(sem("kt_out"), pr * 10 + (5 + u + 1))
                    if b2 == 0 and kt >= 2:
                        pe.wait_ge(sem("s_ev"), pr * 5 + (kt - 1))
                    biased = kt >= 3
                    for a2 in range(2):
                        r0 = 64 * b2 + 32 * a2
                        ins = mm(ps[r0:r0 + 32, bk, :], Qst[:, b2, a2, :], KTs[:, u % 2, a2, :], start=True,
                                 stop=not biased, skip_group_check=True)
                    if biased and b2 == 1:
                        ins = mm(ps[:, bk, :], RB, ohs[:, 0:WIN], start=False, stop=True, skip_group_check=True)
                    ins.then_inc(sem("s_unit"), 1)

                ktr(0)
                for u in range(10):
                    if u < 9:
                        ktr(u + 1)
                    scores(u)
                    if u == 1:
                        pe.wait_ge(sem("pc_ready"), pr + 1)
                        mm(ps[:, 6, 32:32 + NBLK], samekv, Pcs, start=True, stop=True).then_inc(sem("imp_mm"), 1)
                for j in range(2):
                    for b2 in range(2):
                        for a2 in range(2):
                            r0 = 64 * b2 + 32 * a2
                            mm(ps[r0:r0 + 32, 7, 32 * j:32 * j + 32], Qst[:, b2, a2, :], KT[:, j, a2, TP:T],
                               start=True, stop=False, skip_group_check=True)
                    ins = mm(ps[:, 7, 32 * j:32 * j + 32], RB, ohs[:, WIN:WIN + TSN], start=False, stop=True,
                             skip_group_check=True)
                ins.then_inc(sem("s_new"), 1)
                NS = PAST + TSN
                offs = [i * P for i in range(16)] + [NS + i * P for i in range(4)]
                for c in range(5):
                    pe.wait_ge(sem("s_p"), pr * 5 + (c + 1))
                    if c == 4:
                        pe.wait_ge(sem("pt_out"), pr * 6 + 1)
                    for i in range(4):
                        o = offs[4 * c + i]
                        ins = tr(ps[:, c % 4, i * P:(i + 1) * P], Sx[:, o:o + P], ident)
                    ins.then_inc(sem("pt_tr"), 1)
                for j, src in enumerate([Sx[:, PAST:PAST + TSN], Sx[:, NS + WIN:NS + WIN + TSN], Scs]):
                    ins = tr(ps[0:TSN, 4, j * P:(j + 1) * P], src, ident)
                ins.then_inc(sem("pt_tr"), 1)
                pe.wait_ge(sem("pt_out"), pr * 6 + 6)
                pe.wait_ge(sem("v_in"), pr * 640 + 640)
                for b2 in range(2):
                    r = slice(64 * b2, 64 * b2 + 64)
                    dst = ps[r, 5, 0:KVC]
                    for i in range(20):
                        mm(dst, PT[:, i, r], V[:, b2, i, :], start=(i == 0), stop=False)
                    for j in range(2):
                        mm(dst, PTn[:, j, r], kv[0:TSN, 2, (3 + 2 * j) * KVC:(4 + 2 * j) * KVC], start=False, stop=False)
                    ins = mm(dst, PTn[:, 2, r], vcs[:, b2, :], start=False, stop=True)
                ins.then_inc(sem("o_mm"), 1)
                pe.wait_ge(sem("o_ready"), pr + 1)
                tr(ps[:, 4, 0:P], Od.rearrange("p a d -> p (a d)"), ident).then_inc(sem("ot_mm"), 1)
                pe.wait_ge(sem("ot_ev"), pr + 1)
            for j in range(4):
                w = slot(START["wout"] + j).rearrange("p (k n) -> p k n", k=KD)
                for c in range(2):
                    ins = linear(w, c, ps[:, 2 * j + c, 0:T], OT)
                ins.then_inc(slot_used, 1 if j < 3 else 1 + M0 - NPRE)
            pe.wait_ge(sem("wout_done"), 1)
            norm(3, sqM)
            for t, (t0, n) in enumerate(TILES):
                for k in range(KD):
                    operand(k)
                    ins = mm(ps[0:n, 4, 8 * t:8 * t + 8], xnT[:, k, t0:t0 + n], wr[:, k, :], start=(k == 0),
                             stop=(k == KD - 1))
            ins.then_inc(sem("rt_mm"), 1)
            for t, (t0, n) in enumerate(TILES):
                if t == 2:
                    pe.wait_ge(sem("xr_ev"), 1)
                for c in range(KD):
                    ins = tr(ps[0:n, 2 * (t % 2) + c // 4, (c % 4) * P:(c % 4 + 1) * P], xnT[:, c, t0:t0 + n], ident)
                ins.then_inc(sem("xr_mm"), 1)
            pe.wait_ge(sem("mk_ready"), 1)
            for t, (t0, n) in enumerate(TILES):
                for s in range(t + 1):
                    m = TILES[s][1]
                    lhs = before[0:n, 0:n] if s == t else ones[0:m, 0:n]
                    mm(ps[0:n, 5, 8 * t:8 * t + 8], lhs, mk8[0:m, s, :], start=(s == 0), stop=(s == t))
            for s in range(3):
                m = TILES[s][1]
                ins = mm(ps[:, 5, 24:32], ones[0:m, :], mk8[0:m, s, :], start=(s == 0), stop=(s == 2))
            ins.then_inc(sem("pfx_mm"), 1)
            pe.wait_ge(sem("xr_ev"), 3)

            def gather(n_se):
                pe.wait_ge(sem("se_ready"), n_se)
                for c in range(KD):
                    for t, (t0, n) in enumerate(TILES):
                        ins = mm(ps[:, c // 4, (c % 4) * P:(c % 4 + 1) * P], Xn[0:n, t, c * P:(c + 1) * P], Se[0:n, t, :],
                                 start=(t == 0), stop=(t == 2))
                ins.then_inc(sem("xe_mm"), 1)

            def experts(turn):
                def eslot(k):
                    s = k % RING
                    pe.wait_ge(full[s], turn * (16 * per[s]) + (counts[s] + 16 * (k // RING + 1)))
                    return ring[:, s, :]
                pe.wait_ge(sem("xe_ev"), turn + 1)
                for u in range(11):
                    pe.wait_ge(sem("gu_ev"), turn * 11 + (u + 1))
                    bk = 2 + u % 2
                    for j in range(2):
                        w = cols_view(eslot(2 * u + j))
                        for c in range(2):
                            dst = ps[:, bk, (2 * j + c) * P:(2 * j + c + 1) * P]
                            for k in range(KD):
                                ins = mm(dst, w[:, k, c * P:(c + 1) * P], XeT[:, k, :], start=(k == 0), stop=(k == KD - 1))
                        ins.then_inc(slot_used, 1)
                pe.wait_ge(sem("sw_made"), turn + 1)
                for t, (t0, n) in enumerate(TILES):
                    ins = tr(ps[:, 7, t0:t0 + n], Sw[0:n, t, :], ident[0:n, 0:n])
                ins.then_inc(sem("sw_tr"), 1)
                pe.wait_ge(sem("gu_ev"), turn * 11 + 13)
                for k in range(11):
                    w = eslot(22 + k).rearrange("p (k n) -> p k n", k=2)
                    for kk in range(2):
                        for c in range(2):
                            ins = mm(ps[:, 4 + c, :], He[:, 2 * k + kk, :], w[:, kk, 512 * c:512 * (c + 1)],
                                     start=(k == 0 and kk == 0), stop=(k == 10 and kk == 1))
                    ins.then_inc(slot_used, 1 if k < 10 else 1 + EPAD - 33)
                gather(turn + 2)
                pe.wait_ge(sem("y_ev"), turn + 1)
                pe.wait_ge(sem("sw_ready"), turn + 1)
                for j in range(4):
                    if j >= 2:
                        pe.wait_ge(sem("h_ex"), turn * 4 + (j - 1))
                    bk = 6 - 2 * (j % 2)
                    for c in range(2):
                        cc = 2 * j + c
                        ins = mm(ps[:, bk + c, 0:T], Ye[:, cc * P:(cc + 1) * P], SwT, start=True, stop=True)
                    ins.then_inc(sem("o_ex"), 1)

            gather(1)
            pe.sem_inc(sem("gu_ev"), 2)
            pe.sem_inc(sem("o_ex"), 1)
            with pe.Fori(0, NE, 1) as e:
                experts(e)
            pe.wait_ge(sem("flag_ready"), 1)
            over = pe.value_load(flag[0:1, 0:1], min_val=0, max_val=1)
            with pe.If(over):
                with pe.Fori(1, 3, 1) as r:
                    with pe.Fori(0, NE, 1) as e:
                        experts(r * NE + e)
            norm(4, sqM, 4)
            for t, (t0, n) in enumerate(TILES):
                for c in range(KD):
                    operand(c)
                    ins = tr(ps[0:n, 2 + 2 * t + c // 4, (c % 4) * P:(c % 4 + 1) * P], xnT[:, c, t0:t0 + n], ident)
                ins.then_inc(sem("yo_mm"), 1)


ARENA = 207 * 1024

_OUTS = [("y_prompt", (1, TP, D)), ("y_sample", (NB, TS, D)), ("kv_prompt", (1, TP, 4, NKV, HD)),
         ("win_prompt", (1, TP, 2, NKV, HD)), ("conv_prompt", (1, 1, CW - 1, D)), ("kv_sample", (NB, TS, 4, NKV, HD)),
         ("win_sample", (NB, WIN, 2, NKV, HD)), ("conv_sample", (1, NB, CW - 1, D))]


def kernel(**inputs):
    import numpy as _np
    import concourse.bacc as _bacc
    from concourse import mybir as _mybir
    from concourse.bass_utils import run_bass_kernel_spmd as _run

    nc = _bacc.Bacc("TRN2", target_bir_lowering=False, num_devices=1)
    arrays, aps = {}, {}
    for name, x in {**inputs, **constants()}.items():
        x = _np.ascontiguousarray(x)
        arrays["in_" + name] = x
        aps[name] = nc.dram_tensor("in_" + name, x.shape, _mybir.dt.from_np(x.dtype), kind="ExternalInput").ap()
    outs = {name: nc.dram_tensor("out_" + name, shape, F32, kind="ExternalOutput").ap() for name, shape in _OUTS}
    build(nc, aps, outs)
    r = _run(nc, [arrays], core_ids=[0])
    return tuple(r.results[0]["out_" + name] for name, _ in _OUTS)
```
